# Optimizing a Trainium2 kernel written in Bass

```python
import jax
import jax.numpy as jnp
from jax import lax
import numpy as np
import math
import jax, jax.numpy as jnp

D_MODEL = 1024
BATCH = 1
SEQ = 512
DEPTH = 2

HEAD_DIM = 64
RWKV_WIDTH = D_MODEL // 4
RWKV_HEADS = RWKV_WIDTH // HEAD_DIM
RWKV_DECAY_LORA = 64
RWKV_ICLR_LORA = 64
RWKV_GATE_LORA = 128
RWKV_COLS = 3 * RWKV_WIDTH + RWKV_GATE_LORA + 2 * RWKV_DECAY_LORA + 2 * RWKV_ICLR_LORA
MLA_V = 64
MLA_WIDTH = D_MODEL // 2
MLA_HEADS = MLA_WIDTH // MLA_V
MLA_NOPE = 64
MLA_ROPE = 32
MLA_Q_RANK = 384
MLA_KV_RANK = 256
MLA_COLS = MLA_Q_RANK + MLA_KV_RANK + MLA_ROPE
MLA_BLOCK = 128
RET_WIDTH = D_MODEL - RWKV_WIDTH - MLA_WIDTH
RET_HEADS = RET_WIDTH // HEAD_DIM
RET_COLS = 4 * RET_WIDTH
RET_CHUNK = 128

MIX_WIDTH = RWKV_WIDTH + MLA_WIDTH + RET_WIDTH
IN_COLS = RWKV_COLS + MLA_COLS + RET_COLS
D_FF = 2816
N_MOD = 9
ROPE_BASE = 10000.0
NORM_EPS = 1e-6
RWKV_LN_EPS = 64e-5
RET_LN_EPS = 1e-5


def split_cols(t, sizes):
    idx = np.cumsum(sizes)[:-1].tolist()
    return jnp.split(t, idx, axis=-1)

def rms_norm(t, eps=NORM_EPS):
    tf = t.astype(jnp.float32)
    return (tf * lax.rsqrt(jnp.mean(tf * tf, axis=-1, keepdims=True) + eps)).astype(t.dtype)

def head_norm(t, eps):
    tf = t.astype(jnp.float32)
    mu = jnp.mean(tf, axis=-1, keepdims=True)
    var = jnp.mean(jnp.square(tf - mu), axis=-1, keepdims=True)
    return (tf - mu) * lax.rsqrt(var + eps)

def modulate(t, shift, scale):
    return t * (1.0 + scale[:, None, :]) + shift[:, None, :]

def swiglu(h, w_in, w_out):
    gate, up = jnp.split(h @ w_in, 2, axis=-1)
    return (jax.nn.silu(gate) * up) @ w_out

def rotary(t, positions):
    d = t.shape[-1]
    inv = ROPE_BASE ** (-jnp.arange(0, d, 2, dtype=jnp.float32) / d)
    ang = positions.astype(jnp.float32)[..., None] * inv
    ang = ang.reshape(ang.shape[:2] + (1,) * (t.ndim - 3) + ang.shape[-1:])
    cos, sin = jnp.cos(ang).astype(t.dtype), jnp.sin(ang).astype(t.dtype)
    t1, t2 = t[..., : d // 2], t[..., d // 2:]
    return jnp.concatenate([t1 * cos - t2 * sin, t2 * cos + t1 * sin], axis=-1)

def centred_shift(t, mu):
    prev = jnp.pad(t[:, :-1], ((0, 0), (1, 0), (0, 0)))
    nxt = jnp.pad(t[:, 1:], ((0, 0), (0, 1), (0, 0)))
    return t + mu * (0.5 * (prev + nxt) - t)

def _dir_stack(t):
    t = jnp.stack([t[:, :, 0], jnp.flip(t[:, :, 1], axis=1)], axis=2)
    return jnp.transpose(t, (1, 2, 0, 3, 4))

def rwkv7_mixer(z, mu, w0, w_up, a0, a_up, g_up, k_k, k_a, r_k, ln_g, ln_b):
    B, S, _ = z.shape
    H, N = RWKV_HEADS, HEAD_DIM
    z = centred_shift(z, mu)
    r, k, v, g_lo, w_lo, a_lo = split_cols(
        z, [RWKV_WIDTH, RWKV_WIDTH, RWKV_WIDTH, RWKV_GATE_LORA, 2 * RWKV_DECAY_LORA, 2 * RWKV_ICLR_LORA])
    w_lo = w_lo.reshape(B, S, 2, RWKV_DECAY_LORA)
    a_lo = a_lo.reshape(B, S, 2, RWKV_ICLR_LORA)
    w_raw = (w0 + jnp.einsum('bsdr,drc->bsdc', jnp.tanh(w_lo), w_up)).astype(jnp.float32)
    decay = jnp.exp(-jnp.exp(-jax.nn.softplus(-w_raw) - 0.5)).reshape(B, S, 2, H, N)
    a = jax.nn.sigmoid(a0 + jnp.einsum('bsdr,drc->bsdc', a_lo, a_up))
    g = jax.nn.sigmoid(g_lo) @ g_up
    kk = (k * k_k).reshape(B, S, H, N).astype(jnp.float32)
    kk = kk / jnp.maximum(jnp.linalg.norm(kk, axis=-1, keepdims=True), 1e-12)
    kk2 = jnp.broadcast_to(kk[:, :, None], (B, S, 2, H, N))
    a5 = a.reshape(B, S, 2, H, N)
    k_mod = (k[:, :, None, :] * (1.0 + (a - 1.0) * k_a)).reshape(B, S, 2, H, N)
    rh, kh, vh = (t.reshape(B, S, H, N) for t in (r, k, v))
    r2 = jnp.broadcast_to(rh[:, :, None], (B, S, 2, H, N))
    v2 = jnp.broadcast_to(vh[:, :, None], (B, S, 2, H, N))
    xs = tuple(_dir_stack(t) for t in (decay, kk2, kk2 * a5, k_mod, v2, r2))

    def step(state, inp):
        w_t, kk_t, kka_t, k_t, v_t, r_t = inp
        sk = jnp.einsum('dbhvk,dbhk->dbhv', state, kk_t)
        new = (state * w_t[..., None, :] - sk[..., :, None] * kka_t[..., None, :]
               + v_t[..., :, None] * k_t[..., None, :])
        y_fwd = jnp.einsum('bhvk,bhk->bhv', new[0], r_t[0])
        y_bwd = jnp.einsum('bhvk,bhk->bhv', state[1], r_t[1])
        return new, jnp.stack([y_fwd, y_bwd])

    state0 = jnp.zeros((2, B, H, N, N), jnp.float32)
    _, ys = lax.scan(step, state0, xs)
    y = ys[:, 0] + jnp.flip(ys[:, 1], axis=0)
    y = jnp.transpose(y, (1, 0, 2, 3))
    y = (head_norm(y, RWKV_LN_EPS) * ln_g + ln_b).astype(z.dtype)
    bonus = jnp.sum(rh * kh * r_k, axis=-1, keepdims=True) * vh
    return (y + bonus).reshape(B, S, RWKV_WIDTH) * g

def mla_mixer(z, positions, q_norm_g, w_uq, kv_norm_g, w_ukv):
    B, S, _ = z.shape
    H = MLA_HEADS
    cq, ckv, kpe = split_cols(z, [MLA_Q_RANK, MLA_KV_RANK, MLA_ROPE])
    q = ((rms_norm(cq) * q_norm_g) @ w_uq).reshape(B, S, H, MLA_NOPE + MLA_ROPE)
    kv = ((rms_norm(ckv) * kv_norm_g) @ w_ukv).reshape(B, S, H, MLA_NOPE + MLA_V)
    q_nope, q_pe = q[..., :MLA_NOPE], rotary(q[..., MLA_NOPE:], positions)
    k_nope, v = kv[..., :MLA_NOPE], kv[..., MLA_NOPE:]
    k_pe = rotary(kpe, positions)
    scale = (MLA_NOPE + MLA_ROPE) ** -0.5
    nb = S // MLA_BLOCK
    qn_b = jnp.transpose(q_nope.reshape(B, nb, MLA_BLOCK, H, MLA_NOPE), (1, 0, 2, 3, 4))
    qp_b = jnp.transpose(q_pe.reshape(B, nb, MLA_BLOCK, H, MLA_ROPE), (1, 0, 2, 3, 4))

    def attend(blk):
        qn, qp = blk
        s = (jnp.einsum('bqhd,bkhd->bhqk', qn, k_nope)
             + jnp.einsum('bqhr,bkr->bhqk', qp, k_pe))
        p = jax.nn.softmax(s.astype(jnp.float32) * scale, axis=-1).astype(v.dtype)
        return jnp.einsum('bhqk,bkhd->bqhd', p, v)

    o = lax.map(attend, (qn_b, qp_b))
    return jnp.transpose(o, (1, 0, 2, 3, 4)).reshape(B, S, MLA_WIDTH)

def retention_dir(q, k, v, log_gamma, strict):
    B, H, S, d = q.shape
    C = RET_CHUNK
    n = S // C
    qc, kc, vc = (t.reshape(B, H, n, C, d) for t in (q, k, v))
    lg = log_gamma.astype(jnp.float32)
    pos = jnp.arange(C, dtype=jnp.float32)
    diff = pos[:, None] - pos[None, :]
    mask = diff > 0 if strict else diff >= 0
    dmat = jnp.where(mask, jnp.exp(lg[:, None, None] * jnp.maximum(diff, 0.0)), 0.0)
    scores = jnp.einsum('bhncd,bhnmd->bhncm', qc, kc) * dmat[None, :, None]
    inner = jnp.einsum('bhncm,bhnme->bhnce', scores, vc)
    k_w = kc * jnp.exp(lg[:, None] * (C - 1.0 - pos)[None, :])[None, :, None, :, None]
    kv = jnp.einsum('bhncd,bhnce->nbhde', k_w, vc)
    chunk_decay = jnp.exp(lg * C)[None, :, None, None]

    def step(R, kv_n):
        return R * chunk_decay + kv_n, R

    _, r_prev = lax.scan(step, jnp.zeros((B, H, d, d), jnp.float32), kv)
    q_w = qc * jnp.exp(lg[:, None] * (pos + 1.0)[None, :])[None, :, None, :, None]
    cross = jnp.einsum('bhncd,nbhde->bhnce', q_w, r_prev)
    return (inner + cross).reshape(B, H, S, d)

def retention_mixer(z, positions, log_rate, gn_g):
    B, S, _ = z.shape
    H, d = RET_HEADS, HEAD_DIM
    q, k, v, gate = split_cols(z, [RET_WIDTH] * 4)
    q = rotary(q.reshape(B, S, H, d), positions)
    k = rotary(k.reshape(B, S, H, d), positions) * (d ** -0.5)
    v = v.reshape(B, S, H, d)
    q, k, v = (jnp.transpose(t, (0, 2, 1, 3)) for t in (q, k, v))
    log_gamma = -jnp.exp(log_rate.astype(jnp.float32))
    y_f = retention_dir(q, k, v, log_gamma[0], False)
    y_b = jnp.flip(retention_dir(jnp.flip(q, 2), jnp.flip(k, 2), jnp.flip(v, 2), log_gamma[1], True), 2)
    y = jnp.transpose(y_f + y_b, (0, 2, 1, 3))
    y = (head_norm(y, RET_LN_EPS) * gn_g).astype(z.dtype).reshape(B, S, RET_WIDTH)
    return jax.nn.silu(gate) * y

def first_inputs(seed: int = 0) -> dict:
    key = jax.random.key(seed)
    ks = jax.random.split(key, 32)
    L, D = DEPTH, D_MODEL
    C = RWKV_WIDTH

    def nrm(k, shape, scale):
        return jax.random.normal(k, shape, jnp.float32) * scale

    ret_base = jnp.log(2.0 ** (-5.0 - jnp.arange(RET_HEADS, dtype=jnp.float32)))
    return {
        'x': nrm(ks[0], (BATCH, SEQ, D), 1.0),
        'c': nrm(ks[1], (BATCH, D), 1.0),
        'positions': jnp.tile(jnp.arange(SEQ, dtype=jnp.int32)[None, :], (BATCH, 1)),
        'w_ada': nrm(ks[2], (L, D, N_MOD * D), 0.5 * D ** -0.5),
        'b_ada': nrm(ks[3], (L, N_MOD * D), 0.02),
        'w_ff1_in': nrm(ks[4], (L, D, 2 * D_FF), D ** -0.5),
        'w_ff1_out': nrm(ks[5], (L, D_FF, D), D_FF ** -0.5),
        'w_ff2_in': nrm(ks[6], (L, D, 2 * D_FF), D ** -0.5),
        'w_ff2_out': nrm(ks[7], (L, D_FF, D), D_FF ** -0.5),
        'w_in': nrm(ks[8], (L, D, IN_COLS), D ** -0.5),
        'w_out': nrm(ks[9], (L, MIX_WIDTH, D), MIX_WIDTH ** -0.5),
        'rwkv_mu': jax.random.uniform(ks[10], (L, RWKV_COLS), jnp.float32),
        'rwkv_w0': jax.random.uniform(ks[11], (L, 2, C), jnp.float32, minval=-5.0, maxval=1.0),
        'rwkv_w_up': nrm(ks[12], (L, 2, RWKV_DECAY_LORA, C), 0.5 * RWKV_DECAY_LORA ** -0.5),
        'rwkv_a0': nrm(ks[13], (L, 2, C), 0.5),
        'rwkv_a_up': nrm(ks[14], (L, 2, RWKV_ICLR_LORA, C), 0.5 * RWKV_ICLR_LORA ** -0.5),
        'rwkv_g_up': nrm(ks[15], (L, RWKV_GATE_LORA, C), RWKV_GATE_LORA ** -0.5),
        'rwkv_k_k': 0.85 + nrm(ks[16], (L, C), 0.05),
        'rwkv_k_a': 1.0 + nrm(ks[17], (L, C), 0.05),
        'rwkv_r_k': nrm(ks[18], (L, RWKV_HEADS, HEAD_DIM), 0.1),
        'rwkv_ln_g': 1.0 + nrm(ks[19], (L, RWKV_HEADS, HEAD_DIM), 0.05),
        'rwkv_ln_b': nrm(ks[20], (L, RWKV_HEADS, HEAD_DIM), 0.02),
        'mla_q_norm_g': 1.0 + nrm(ks[21], (L, MLA_Q_RANK), 0.05),
        'mla_w_uq': nrm(ks[22], (L, MLA_Q_RANK, MLA_HEADS * (MLA_NOPE + MLA_ROPE)), MLA_Q_RANK ** -0.5),
        'mla_kv_norm_g': 1.0 + nrm(ks[23], (L, MLA_KV_RANK), 0.05),
        'mla_w_ukv': nrm(ks[24], (L, MLA_KV_RANK, MLA_HEADS * (MLA_NOPE + MLA_V)), MLA_KV_RANK ** -0.5),
        'ret_log_rate': ret_base + nrm(ks[25], (L, 2, RET_HEADS), 0.1),
        'ret_gn_g': 1.0 + nrm(ks[26], (L, RET_HEADS, HEAD_DIM), 0.05),
        'final_norm_g': 1.0 + nrm(ks[27], (D,), 0.05),
    }

def first_block(x, c, positions, w_ada, b_ada, w_ff1_in, w_ff1_out, w_ff2_in, w_ff2_out,
              w_in, w_out, rwkv_mu, rwkv_w0, rwkv_w_up, rwkv_a0, rwkv_a_up, rwkv_g_up,
              rwkv_k_k, rwkv_k_a, rwkv_r_k, rwkv_ln_g, rwkv_ln_b, mla_q_norm_g, mla_w_uq,
              mla_kv_norm_g, mla_w_ukv, ret_log_rate, ret_gn_g, final_norm_g):
    cond = jax.nn.silu(c)
    for l in range(DEPTH):
        mod = cond @ w_ada[l] + b_ada[l]
        sh1, sc1, g1, sh2, sc2, g2, sh3, sc3, g3 = jnp.split(mod, N_MOD, axis=-1)
        h = modulate(rms_norm(x), sh1, sc1)
        x = x + 0.5 * g1[:, None, :] * swiglu(h, w_ff1_in[l], w_ff1_out[l])
        h = modulate(rms_norm(x), sh2, sc2)
        z = h @ w_in[l]
        z_a, z_b, z_c = split_cols(z, [RWKV_COLS, MLA_COLS, RET_COLS])
        o_a = rwkv7_mixer(z_a, rwkv_mu[l], rwkv_w0[l], rwkv_w_up[l], rwkv_a0[l], rwkv_a_up[l],
                          rwkv_g_up[l], rwkv_k_k[l], rwkv_k_a[l], rwkv_r_k[l], rwkv_ln_g[l], rwkv_ln_b[l])
        o_b = mla_mixer(z_b, positions, mla_q_norm_g[l], mla_w_uq[l], mla_kv_norm_g[l], mla_w_ukv[l])
        o_c = retention_mixer(z_c, positions, ret_log_rate[l], ret_gn_g[l])
        mixed = jnp.concatenate([o_a, o_b, o_c], axis=-1) @ w_out[l]
        x = x + g2[:, None, :] * mixed
        h = modulate(rms_norm(x), sh3, sc3)
        x = x + 0.5 * g3[:, None, :] * swiglu(h, w_ff2_in[l], w_ff2_out[l])
    return rms_norm(x) * final_norm_g


CHUNK = 64
D_MIX = D_MODEL
POOL_WIDTH = D_MIX // 4
DIFF_WIDTH = D_MIX // 2
GLA_WIDTH = D_MIX // 4
POOL_WINDOWS = (2, 4, 8, 16)
POOL_GROUPS = len(POOL_WINDOWS)
POOL_GDIM = POOL_WIDTH // POOL_GROUPS
DIFF_HEADS = 4
DIFF_VDIM = DIFF_WIDTH // DIFF_HEADS
DIFF_QKDIM = DIFF_VDIM // 2
GLA_HEADS = 4
GLA_VDIM = GLA_WIDTH // GLA_HEADS
GLA_KDIM = GLA_VDIM // 2
GLA_GATE_RANK = 16
GLA_GATE_TAU = 16.0
D_FF_2 = 4 * D_MODEL
Q_BLOCK = 128
EPS = 1e-6

SIZES = (
    POOL_WIDTH,
    DIFF_HEADS * 2 * DIFF_QKDIM,
    DIFF_HEADS * 2 * DIFF_QKDIM,
    DIFF_HEADS * DIFF_VDIM,
    GLA_HEADS * GLA_KDIM,
    GLA_HEADS * GLA_KDIM,
    GLA_WIDTH,
    GLA_WIDTH,
    GLA_GATE_RANK,
)
D_IN_PROJ = sum(SIZES)
SPLIT_POINTS = tuple(sum(SIZES[:i + 1]) for i in range(len(SIZES) - 1))


def rms_norm_2(x, g):
    xf = x.astype(jnp.float32)
    y = xf * lax.rsqrt(jnp.mean(xf * xf, axis=-1, keepdims=True) + EPS)
    return (y * g.astype(jnp.float32)).astype(x.dtype)

def pool_mixer(u, w_pool, pool_scale):
    B, S, _ = u.shape
    uf = u.astype(jnp.float32).reshape(B, S, POOL_GROUPS, POOL_GDIM)
    csum = jnp.cumsum(uf, axis=1)
    t = jnp.arange(S)
    means = []
    for g, win in enumerate(POOL_WINDOWS):
        c = csum[:, :, g]
        c_prev = jnp.pad(c, ((0, 0), (win, 0), (0, 0)))[:, :S]
        cnt = jnp.minimum(t + 1, win).astype(jnp.float32)[None, :, None]
        means.append((c - c_prev) / cnt)
    pooled = jnp.stack(means, axis=2) - uf
    mixed = jnp.einsum('bsgc,gcd->bsgd', pooled, w_pool.astype(jnp.float32))
    return (mixed.reshape(B, S, POOL_WIDTH) * pool_scale.astype(jnp.float32)).astype(u.dtype)

def diff_attention(q, k, v, lq1, lk1, lq2, lk2, norm_g, lambda_init):
    B, S = q.shape[:2]
    nqb = S // Q_BLOCK
    f32 = jnp.float32
    lam = (jnp.exp(jnp.sum(lq1.astype(f32) * lk1.astype(f32)))
           - jnp.exp(jnp.sum(lq2.astype(f32) * lk2.astype(f32))) + lambda_init)
    scale = DIFF_QKDIM ** -0.5
    k_chunk = jnp.arange(S) // CHUNK
    qb = q.reshape(B, nqb, Q_BLOCK, DIFF_HEADS, 2, DIFF_QKDIM).transpose(1, 0, 2, 3, 4, 5)

    def one_block(args):
        q_blk, blk = args
        s = jnp.einsum('bqhmd,bkhmd->bhmqk', q_blk, k).astype(f32) * scale
        q_chunk = (blk * Q_BLOCK + jnp.arange(Q_BLOCK)) // CHUNK
        mask = k_chunk[None, :] <= q_chunk[:, None]
        s = jnp.where(mask, s, -jnp.inf)
        p = jax.nn.softmax(s, axis=-1)
        a = p[:, :, 0] - lam * p[:, :, 1]
        return jnp.einsum('bhqk,bkhd->bqhd', a.astype(v.dtype), v)

    o = lax.map(one_block, (qb, jnp.arange(nqb)))
    o = o.transpose(1, 0, 2, 3, 4).reshape(B, S, DIFF_HEADS, DIFF_VDIM)
    o = rms_norm_2(o, norm_g.reshape(DIFF_HEADS, DIFF_VDIM)) * (1.0 - lambda_init)
    return o.reshape(B, S, DIFF_WIDTH)

def gla_mixer(q, k, v, r, g_lr, w_gate2, b_gate, norm_g):
    B, S = q.shape[:2]
    nc = S // CHUNK
    f32 = jnp.float32
    log_a = jax.nn.log_sigmoid((g_lr @ w_gate2 + b_gate).astype(f32)) / GLA_GATE_TAU
    log_a = log_a.reshape(B, S, GLA_HEADS, GLA_KDIM)

    def to_chunks(t):
        return t.astype(f32).reshape(B, nc, CHUNK, GLA_HEADS, t.shape[-1]).transpose(1, 0, 3, 2, 4)

    qc = to_chunks(q) * (GLA_KDIM ** -0.5)
    kc, vc, lc = to_chunks(k), to_chunks(v), to_chunks(log_a)
    bcum = jnp.cumsum(lc, axis=3)
    b_last = bcum[:, :, :, -1, :]
    q_dec = qc * jnp.exp(bcum)
    k_inv = kc * jnp.exp(-bcum)
    k_end = kc * jnp.exp(b_last[:, :, :, None, :] - bcum)
    causal = jnp.tril(jnp.ones((CHUNK, CHUNK), dtype=bool))
    att = jnp.where(causal, jnp.einsum('nbhid,nbhjd->nbhij', q_dec, k_inv), 0.0)
    o_intra = jnp.einsum('nbhij,nbhje->nbhie', att, vc)

    def step(state, xs):
        q_d, k_e, v_c, decay = xs
        o_inter = jnp.einsum('bhid,bhde->bhie', q_d, state)
        state = state * jnp.exp(decay)[..., None] + jnp.einsum('bhjd,bhje->bhde', k_e, v_c)
        return state, o_inter

    state0 = jnp.zeros((B, GLA_HEADS, GLA_KDIM, GLA_VDIM), f32)
    _, o_inter = lax.scan(step, state0, (q_dec, k_end, vc, b_last))
    o = (o_intra + o_inter).transpose(1, 0, 3, 2, 4).reshape(B, S, GLA_HEADS, GLA_VDIM)
    o = rms_norm_2(o, norm_g.reshape(GLA_HEADS, GLA_VDIM)).reshape(B, S, GLA_WIDTH)
    return (o * jax.nn.silu(r.astype(f32))).astype(r.dtype)

def second_inputs(seed: int = 0) -> dict:
    key = jax.random.key(seed)
    ks = jax.random.split(key, 24)
    nrm = jax.random.normal
    f32 = jnp.float32
    L = DEPTH
    return {
        "x": nrm(ks[0], (BATCH, SEQ, D_MODEL), f32),
        "norm1_g": 1.0 + 0.05 * nrm(ks[1], (L, D_MODEL), f32),
        "w_in": nrm(ks[2], (L, D_MODEL, D_IN_PROJ), f32) * D_MODEL ** -0.5,
        "pool_w": nrm(ks[3], (L, POOL_GROUPS, POOL_GDIM, POOL_GDIM), f32) * POOL_GDIM ** -0.5,
        "pool_scale": 1.0 + 0.1 * nrm(ks[4], (L, POOL_WIDTH), f32),
        "diff_lq1": 0.1 * nrm(ks[5], (L, DIFF_QKDIM), f32),
        "diff_lk1": 0.1 * nrm(ks[6], (L, DIFF_QKDIM), f32),
        "diff_lq2": 0.1 * nrm(ks[7], (L, DIFF_QKDIM), f32),
        "diff_lk2": 0.1 * nrm(ks[8], (L, DIFF_QKDIM), f32),
        "diff_norm_g": 1.0 + 0.05 * nrm(ks[9], (L, DIFF_WIDTH), f32),
        "gla_w_gate2": nrm(ks[10], (L, GLA_GATE_RANK, GLA_HEADS * GLA_KDIM), f32) * GLA_GATE_RANK ** -0.5,
        "gla_b_gate": 0.1 * nrm(ks[11], (L, GLA_HEADS * GLA_KDIM), f32),
        "gla_norm_g": 1.0 + 0.05 * nrm(ks[12], (L, GLA_WIDTH), f32),
        "w_out": nrm(ks[13], (L, D_MIX, D_MODEL), f32) * D_MIX ** -0.5,
        "norm2_g": 1.0 + 0.05 * nrm(ks[14], (L, D_MODEL), f32),
        "w_mlp1": nrm(ks[15], (L, D_MODEL, D_FF_2), f32) * D_MODEL ** -0.5,
        "w_mlp2": nrm(ks[16], (L, D_FF_2, D_MODEL), f32) * D_FF_2 ** -0.5,
        "final_norm_g": 1.0 + 0.05 * nrm(ks[17], (D_MODEL,), f32),
    }

def second_block(x, norm1_g, w_in, pool_w, pool_scale, diff_lq1, diff_lk1, diff_lq2, diff_lk2,
              diff_norm_g, gla_w_gate2, gla_b_gate, gla_norm_g, w_out, norm2_g, w_mlp1,
              w_mlp2, final_norm_g):
    B, S, _ = x.shape
    h = x
    for l in range(DEPTH):
        u = rms_norm_2(h, norm1_g[l])
        proj = u @ w_in[l]
        p_in, dq, dk, dv, gq, gk, gv, gr, gg = jnp.split(proj, SPLIT_POINTS, axis=-1)
        y_pool = pool_mixer(p_in, pool_w[l], pool_scale[l])
        lambda_init = 0.8 - 0.6 * math.exp(-0.3 * l)
        y_diff = diff_attention(
            dq.reshape(B, S, DIFF_HEADS, 2, DIFF_QKDIM),
            dk.reshape(B, S, DIFF_HEADS, 2, DIFF_QKDIM),
            dv.reshape(B, S, DIFF_HEADS, DIFF_VDIM),
            diff_lq1[l], diff_lk1[l], diff_lq2[l], diff_lk2[l], diff_norm_g[l], lambda_init)
        y_gla = gla_mixer(
            gq.reshape(B, S, GLA_HEADS, GLA_KDIM),
            gk.reshape(B, S, GLA_HEADS, GLA_KDIM),
            gv.reshape(B, S, GLA_HEADS, GLA_VDIM),
            gr, gg, gla_w_gate2[l], gla_b_gate[l], gla_norm_g[l])
        mix = jnp.concatenate([y_pool, y_diff.astype(y_pool.dtype), y_gla.astype(y_pool.dtype)], axis=-1)
        h = h + (mix @ w_out[l]).astype(h.dtype)
        z = rms_norm_2(h, norm2_g[l])
        h = h + jnp.square(jax.nn.relu(z @ w_mlp1[l])) @ w_mlp2[l]
    return rms_norm_2(h, final_norm_g)


def setup_inputs(seed=0):
    out = dict(first_inputs(seed))
    for name, value in second_inputs(seed + 1).items():
        if name != "x":
            out[name + "_2"] = value
    return out


def reference(
    x, c, positions, w_ada, b_ada, w_ff1_in, w_ff1_out, w_ff2_in, w_ff2_out, w_in, w_out,
    rwkv_mu, rwkv_w0, rwkv_w_up, rwkv_a0, rwkv_a_up, rwkv_g_up, rwkv_k_k, rwkv_k_a, rwkv_r_k,
    rwkv_ln_g, rwkv_ln_b, mla_q_norm_g, mla_w_uq, mla_kv_norm_g, mla_w_ukv, ret_log_rate,
    ret_gn_g, final_norm_g, norm1_g_2, w_in_2, pool_w_2, pool_scale_2, diff_lq1_2, diff_lk1_2,
    diff_lq2_2, diff_lk2_2, diff_norm_g_2, gla_w_gate2_2, gla_b_gate_2, gla_norm_g_2, w_out_2,
    norm2_g_2, w_mlp1_2, w_mlp2_2, final_norm_g_2,
):
    x = first_block(
        x, c, positions, w_ada, b_ada, w_ff1_in, w_ff1_out, w_ff2_in, w_ff2_out, w_in, w_out,
        rwkv_mu, rwkv_w0, rwkv_w_up, rwkv_a0, rwkv_a_up, rwkv_g_up, rwkv_k_k, rwkv_k_a,
        rwkv_r_k, rwkv_ln_g, rwkv_ln_b, mla_q_norm_g, mla_w_uq, mla_kv_norm_g, mla_w_ukv,
        ret_log_rate, ret_gn_g, final_norm_g,
    )
    return second_block(
        x, norm1_g_2, w_in_2, pool_w_2, pool_scale_2, diff_lq1_2, diff_lk1_2, diff_lq2_2,
        diff_lk2_2, diff_norm_g_2, gla_w_gate2_2, gla_b_gate_2, gla_norm_g_2, w_out_2,
        norm2_g_2, w_mlp1_2, w_mlp2_2, final_norm_g_2,
    )


_drawn_inputs = setup_inputs


def setup_inputs(seed=0):
    import zlib

    import numpy as np

    out = dict(_drawn_inputs(seed))
    spreads = {}
    factors = {'rwkv_w_up': 5.267,
     'rwkv_k_k': 3.729,
     'rwkv_k_a': 2.838,
     'rwkv_ln_g': 6.105,
     'rwkv_ln_b': 8.0,
     'mla_q_norm_g': 8.0,
     'mla_kv_norm_g': 3.487,
     'ret_gn_g': 5.862,
     'diff_lq2_2': 5.868,
     'gla_b_gate_2': 3.4,
     'gla_norm_g_2': 3.183}
    for name, (base, spread) in spreads.items():
        noise = np.random.default_rng([zlib.crc32(name.encode()), seed]).standard_normal(out[name].shape)
        drawn = base * np.exp(spread * noise) if base else spread * noise
        out[name] = jnp.asarray(drawn.astype(out[name].dtype))
    for name, factor in factors.items():
        out[name] = (out[name] * factor).astype(out[name].dtype)
    return out
```

```python
from contextlib import ExitStack

import concourse.bass as bass
from concourse import mybir

F32 = mybir.dt.float32
F32R = mybir.dt.float32r
I32 = mybir.dt.int32
ALU = mybir.AluOpType
ACT = mybir.ActivationFunctionType
AX = mybir.AxisListType.X

P = 128
S = 512
D = 1024
DT = D // P
DEPTH = 2
EPS = 1e-6

D_FF = 2816
N_MOD = 9
RW, RW_HEADS, HD = 256, 4, 64
RW_COLS = 1152
MLA_Q, MLA_KV, MLA_ROPE = 384, 256, 32
MLA_HEADS, MLA_NOPE, MLA_V = 8, 64, 64
MLA_QK = MLA_NOPE + MLA_ROPE
MLA_COLS = MLA_Q + MLA_KV + MLA_ROPE
RET_HEADS = 4
ROPE_BASE = 10000.0
D_MLP = 4096
CHUNK = 64
NCH = S // CHUNK
POOL_WINDOWS = (2, 4, 8, 16)
GLA_KD, GLA_RANK, GLA_TAU = 32, 16, 16.0

KC = 8
MC = 2 * P

VECS_1 = [("b_ada", 72), ("rwkv_mu", 9), ("rwkv_w0", 4), ("rwkv_a0", 4), ("rwkv_k_k", 2), ("rwkv_k_a", 2),
          ("rwkv_r_k", 2), ("rwkv_ln_g", 2), ("rwkv_ln_b", 2), ("mla_q_norm_g", 3), ("mla_kv_norm_g", 2),
          ("ret_gn_g", 2)]
VECS_2 = [("norm1_g_2", 8), ("pool_scale_2", 2), ("diff_norm_g_2", 4), ("gla_b_gate_2", 1), ("gla_norm_g_2", 2),
          ("norm2_g_2", 8)]


def places(vecs):
    at, n = {}, 0
    for name, rows in vecs:
        at[name] = n
        n += rows
    return at, n


AT_1, N_VEC_1 = places(VECS_1)
AT_2, N_VEC_2 = places(VECS_2)


class Phases:

    def __init__(self, nc, ctx, size):
        self.nc = nc
        self.sets = [[ctx.enter_context(nc.semaphore(f"set{i}_{j}")) for j in range(size)] for i in (0, 1)]
        self.turn = 0

    def open(self, count):
        self.old = self.sets[1 - self.turn]
        mine = self.sets[self.turn]
        self.turn = 1 - self.turn
        assert count <= len(mine), count
        return mine[:count]

    def clear(self, eng):
        nums = [s.num for s in self.old]
        assert nums == list(range(nums[0], nums[0] + len(nums)))
        eng.sem_clear(range(nums[0], nums[-1] + 1))


def bcast_rows(ap, rows):
    return ap.to_broadcast([rows, ap.shape[-1]])


def constants(nc, k, ph, inv_freq):
    load, built, turned, folded, sines, xload, xt, xdone, cdone, gset, pset = ph.open(11)
    with ExitStack() as ctx:
        def sb(name, shape, dt=F32):
            return ctx.enter_context(nc.sbuf_tensor(name, shape, dt))

        pos_i = sb("pos_i", [P, S], I32)
        inv = sb("inv", [P, 2])
        ang = sb("ang", [P, 2, S])
        turns = sb("turns", [P, 2, S])
        over = sb("over", [P, 2, S])
        xin = sb("xin", [P, 4, D])
        blocks = sb("blocks", [P, 7, P])
        rows = sb("rows", [24, P])
        th = sb("th", [P, 8])
        ps = [ctx.enter_context(nc.psum_tensor(f"ps_const{i}", [P, 512], F32)) for i in (0, 1, 2)]
        block = ctx.enter_context(nc.Block())

        @block.sync
        def _(eng):
            eng.dma_start(pos_i[:, :], bcast_rows(k.inp["positions"], P)).then_inc(load, 16)
            eng.dma_start(inv[:, :], inv_freq).then_inc(load, 16)
            eng.dma_start(rows[0:8, :], k.inp["c"].rearrange("a (r p) -> (a r) p", p=P)).then_inc(load, 16)
            eng.dma_start(rows[8:16, :], k.inp["final_norm_g"].rearrange("(r p) -> r p", p=P)).then_inc(load, 16)
            eng.dma_start(rows[16:24, :], k.inp["final_norm_g_2"].rearrange("(r p) -> r p", p=P)).then_inc(load, 16)
            eng.dma_start(xin[:, :, :], k.inp["x"].rearrange("b (t p) d -> p (b t) d", p=P)).then_inc(xload, 16)

        @block.gpsimd
        def _(eng):
            ph.clear(eng)
            n = 0

            def fill(ap, value):
                nonlocal n
                if n:
                    eng.wait_ge(gset, n)
                eng.memset(ap, value).then_inc(gset, 1)
                n += 1

            def diag(ap, base, size, value):
                nonlocal n
                eng.wait_ge(gset, n)
                eng.affine_select(out=ap, in_=ap, compare_op=ALU.not_equal, fill=value, base=base,
                                  pattern=[[-1, size]], channel_multiplier=1).then_inc(gset, 1)
                n += 1

            for tile in (k.ident, k.rot64, k.rot32, k.put32, k.putrot32):
                fill(tile, 0.0)
            diag(k.ident, 0, P, 1.0)
            for h in (0, 64):
                diag(k.rot64[:, h:h + 32], -h - 32, 32, -1.0)
                diag(k.rot64[:, h + 32:h + 64], -h, 32, 1.0)
            diag(k.rot32[:, 64:80], -80, 16, -1.0)
            diag(k.rot32[:, 80:96], -64, 16, 1.0)
            diag(k.put32[:, 64:96], 0, 32, 1.0)
            diag(k.putrot32[:, 64:80], -16, 16, -1.0)
            diag(k.putrot32[:, 80:96], 0, 16, 1.0)
            fill(k.sum64, 0.0)
            eng.wait_ge(gset, n)
            fill(k.sum64[0:64, 0:64], 1.0)
            fill(k.sum64[64:128, 64:128], 1.0)
            fill(k.ones, 1.0)
            for tile, op_base in ((k.upper, -1), (k.upper_in, 0)):
                fill(tile, 0.0)
                for c in (0, 64):
                    eng.wait_ge(gset, n)
                    fill(tile[c:c + 64, c:c + 64], 1.0)
                eng.wait_ge(gset, n)
                eng.affine_select(out=tile, in_=tile, compare_op=ALU.is_ge, fill=0.0, base=op_base,
                                  pattern=[[1, P]], channel_multiplier=-1).then_inc(gset, 1)
                n += 1
            for tile, op_base in ((k.lower, -1), (k.lower_in, 0)):
                fill(tile, 0.0)
                for c in (0, 64):
                    eng.wait_ge(gset, n)
                    fill(tile[c:c + 64, c:c + 64], 1.0)
                eng.wait_ge(gset, n)
                eng.affine_select(out=tile, in_=tile, compare_op=ALU.is_ge, fill=0.0, base=op_base,
                                  pattern=[[-1, P]], channel_multiplier=1).then_inc(gset, 1)
                n += 1
            for tile, at in ((k.keep_f, 0), (k.keep_b, CHUNK - 1)):
                fill(tile, 1.0)
                eng.wait_ge(gset, n)
                fill(tile.rearrange("p (c t) -> p c t", t=CHUNK)[:, :, at:at + 1], 0.0)
            for lv in range(7):
                w = 2 ** lv
                b = blocks[:, lv, :]
                fill(b, 1.0)
                for base, pat, mul in ((0, [[-w, P // w], [0, w]], 1), (w - 1, [[w, P // w], [0, w]], -1)):
                    eng.wait_ge(gset, n)
                    eng.affine_select(out=b.rearrange("p (b w) -> p b w", w=w), in_=b.rearrange("p (b w) -> p b w", w=w),
                                      compare_op=ALU.is_ge, fill=0.0, base=base, pattern=pat, channel_multiplier=mul)\
                       .then_inc(gset, 1)
                    n += 1
            eng.wait_ge(gset, n)
            eng.tensor_tensor(k.between, blocks[:, 1:7, :], blocks[:, 0:6, :], ALU.subtract).then_inc(gset, 1)
            n += 1
            fill(k.eye64, 0.0)
            diag(k.eye64, 0, 64, 1.0)
            diag(k.eye64, -64, 64, 1.0)
            for tile, cols, value in ((k.mask_q, slice(0, 64), 1.0), (k.mask_k, slice(64, P), -1e30)):
                fill(tile, 0.0)
                for row in (0, 64):
                    fill(tile[row:row + 1, cols], value)
            fill(k.eps[:, 0:1], EPS)
            fill(k.eps[:, 1:2], 64e-5)
            fill(k.eps[:, 2:3], 1e-5)
            fill(k.eps[:, 3:4], 0.0)
            eng.wait_ge(gset, n)
            eng.memset(k.eps[:, 3:4], 0.0).then_inc(built, 1)

        @block.tensor
        def _(eng):
            eng.wait_ge(built, 1)
            eng.wait_ge(load, 80)
            eng.transpose(ps[2][:, 0:24], rows[:, :], k.ident[0:24, 0:24]).then_inc(turned, 1)
            eng.wait_ge(xload, 16)
            for t in range(DT):
                if t >= 2:
                    eng.wait_ge(xdone, t - 1)
                for j in range(4):
                    mm = eng.transpose(ps[t % 2][:, j * P:(j + 1) * P], xin[:, j, t * P:(t + 1) * P], k.ident)
                mm.then_inc(xt, 1)

        @block.scalar
        def _(eng):
            eng.wait_ge(folded, 1)
            eng.activation(k.sin, ang[:, :, :], ACT.Sin).then_inc(sines, 1)
            eng.activation(k.cos, turns[:, :, :], ACT.Sin).then_inc(sines, 1)
            eng.wait_ge(cdone, 1)
            eng.activation(th[:, :], k.cond, ACT.Tanh, scale=0.5).then_inc(sines, 1)

        @block.vector
        def _(eng):
            n = 0

            def then(ins):
                nonlocal n
                ins.then_inc(pset, 1)
                n += 1
                eng.wait_ge(pset, n)

            eng.wait_ge(load, 80)
            then(eng.tensor_copy(over[:, 0, :], pos_i[:, :]))
            for i in (0, 1):
                then(eng.tensor_scalar(ang[:, i, :], over[:, 0, :], inv[:, i:i + 1], None, ALU.mult))
            then(eng.tensor_scalar(turns[:, :, :], ang[:, :, :], 1.0 / (2.0 * np_pi()), 12582912.0, ALU.mult, ALU.add))
            then(eng.tensor_scalar(turns[:, :, :], turns[:, :, :], 12582912.0, None, ALU.subtract))
            for part in two_pi_parts():
                then(eng.scalar_tensor_tensor(out=ang[:, :, :], in0=turns[:, :, :], scalar=-part, in1=ang[:, :, :],
                                              op0=ALU.mult, op1=ALU.add))
            lim = 3.1415925
            then(eng.tensor_scalar(ang[:, :, :], ang[:, :, :], lim, -lim, ALU.min, ALU.max))
            then(eng.tensor_scalar(turns[:, :, :], ang[:, :, :], np_pi() / 2, None, ALU.add))
            then(eng.tensor_scalar(over[:, :, :], turns[:, :, :], np_pi(), -2.0 * np_pi(), ALU.is_gt, ALU.mult))
            then(eng.tensor_tensor(turns[:, :, :], turns[:, :, :], over[:, :, :], ALU.add))
            eng.tensor_scalar(turns[:, :, :], turns[:, :, :], lim, -lim, ALU.min, ALU.max).then_inc(folded, 1)
            for t in range(DT):
                eng.wait_ge(xt, t + 1)
                eng.tensor_copy(k.x[:, t, :], ps[t % 2][:, :]).then_inc(xdone, 1)
            eng.wait_ge(turned, 1)
            eng.tensor_copy(k.cond, ps[2][:, 0:8]).then_inc(cdone, 1)
            eng.tensor_copy(k.finals, ps[2][:, 8:24]).then_inc(cdone, 1)
            eng.wait_ge(sines, 3)
            then(eng.tensor_scalar(th[:, :], th[:, :], 1.0, 0.5, ALU.add, ALU.mult))
            then(eng.tensor_tensor(k.cond, k.cond, th[:, :], ALU.mult))


def np_pi():
    return 3.141592653589793


def two_pi_parts():
    a = 6.28125
    b = 0.0019350051879882812
    return a, b, 2.0 * np_pi() - a - b


def load_vectors(nc, k, ph, l, vecs, n_vec, out, also=None):
    load, turned, copied, halved = ph.open(4)
    with ExitStack() as ctx:
        rows = ctx.enter_context(nc.sbuf_tensor(f"rows_{n_vec}", [n_vec, P], F32))
        ps = ctx.enter_context(nc.psum_tensor(f"ps_rows_{n_vec}", [P, 512], F32))
        block = ctx.enter_context(nc.Block())

        @block.gpsimd
        def _(eng):
            ph.clear(eng)

        @block.sync
        def _(eng):
            at = 0
            for name, r in vecs:
                src = k.flat[name][bass.ds(l, 1), :].rearrange("a (r p) -> (a r) p", p=P)
                eng.dma_start(rows[at:at + r, :], src).then_inc(load, 16)
                at += r

        @block.tensor
        def _(eng):
            eng.wait_ge(load, 16 * len(vecs))
            eng.transpose(ps[:, 0:n_vec], rows[:, :], k.ident[0:n_vec, 0:n_vec]).then_inc(turned, 1)

        @block.vector
        def _(eng):
            eng.wait_ge(turned, 1)
            eng.tensor_copy(out, ps[:, 0:n_vec]).then_inc(copied, 1)
            if also:
                eng.wait_ge(copied, 1)
                also([halved])(eng)


class Side:
    RING, ACC = 2, 6

    def __init__(self, nc, k, ctx, name, sems, l, tiles, finish):
        self.k, self.l, self.tiles, self.finish = k, l, tiles, finish
        self.step, self.summed, self.turned, self.taken, *self.landed = sems
        self.raw = ctx.enter_context(nc.sbuf_tensor(f"{name}_raw", [P, self.RING, KC, P], F32))
        self.acc = ctx.enter_context(nc.sbuf_tensor(f"{name}_acc", [P, self.ACC, P], F32))
        self.ps = [ctx.enter_context(nc.psum_tensor(f"{name}_ps{i}", [P, 512], F32)) for i in (0, 1)]
        self.steps = 0

    SEMS = 4 + RING

    def load(self, eng, s):
        if s >= self.RING:
            eng.wait_ge(self.summed, s - self.RING + 1)
        w = self.k.inp["w_ada"][bass.ds(self.l, 1), :, self.tiles[s] * P:(self.tiles[s] + 1) * P]
        eng.dma_start(self.raw[:, s % self.RING, :, :], w.rearrange("a (q p) n -> p (a q) n", p=P))\
           .then_inc(self.landed[s % self.RING], 16)

    def sum(self, eng, s):
        raw, a, cond = self.raw[:, s % self.RING, :, :], self.acc[:, s % self.ACC, :], self.k.cond
        eng.wait_ge(self.landed[s % self.RING], 16 * (s // self.RING + 1))
        if s >= self.ACC:
            eng.wait_ge(self.turned, s - self.ACC + 1)
        eng.tensor_scalar(a, raw[:, 0, :], cond[:, 0:1], None, ALU.mult).then_inc(self.step, 1)
        self.steps += 1
        for q in range(1, KC):
            eng.wait_ge(self.step, self.steps)
            ins = eng.scalar_tensor_tensor(out=a, in0=raw[:, q, :], scalar=cond[:, q:q + 1], in1=a,
                                           op0=ALU.mult, op1=ALU.add)
            ins.then_inc(self.step if q < KC - 1 else self.summed, 1)
            self.steps += q < KC - 1

    def turn(self, eng, s):
        b, c = s // 4, s % 4
        if b >= 2 and c == 0:
            eng.wait_ge(self.taken, b - 1)
        eng.wait_ge(self.summed, s + 1)
        eng.matmul(self.ps[b % 2][:, c * P:(c + 1) * P], self.acc[:, s % self.ACC, :], self.k.ones,
                   start=True, stop=True).then_inc(self.turned, 1)

    def take(self, eng, b):
        eng.wait_ge(self.turned, 4 * b + 4)
        ps = self.ps[b % 2][:, :].rearrange("p (c n) -> p c n", n=P)[:, :, 0]
        self.finish(eng, 4 * b, ps).then_inc(self.taken, 1)


def first_modulation(nc, k, ph, l, tiles, finish):
    sems = ph.open(Side.SEMS)
    with ExitStack() as ctx:
        side = Side(nc, k, ctx, "ada0", sems, l, tiles, finish)
        block = ctx.enter_context(nc.Block())

        @block.gpsimd
        def _(eng):
            ph.clear(eng)

        @block.sync
        def _(eng):
            for s in range(len(tiles)):
                side.load(eng, s)

        @block.vector
        def _(eng):
            for s in range(len(tiles)):
                side.sum(eng, s)
                if s % 4 == 1 and s > 4:
                    side.take(eng, s // 4 - 1)
            side.take(eng, len(tiles) // 4 - 1)

        @block.tensor
        def _(eng):
            for s in range(len(tiles)):
                side.turn(eng, s)


def normalise(nc, k, ph, name, gain):
    squared, added, logged, inv_ready, scaled = ph.open(5)
    with ExitStack() as ctx:
        sq = ctx.enter_context(nc.sbuf_tensor(f"{name}_sq", [P, DT, S], F32))
        rstd = ctx.enter_context(nc.sbuf_tensor(f"{name}_rstd", [P, S], F32))
        ps = ctx.enter_context(nc.psum_tensor(f"{name}_ps", [P, 512], F32))
        block = ctx.enter_context(nc.Block())

        @block.gpsimd
        def _(eng):
            ph.clear(eng)

        @block.tensor
        def _(eng):
            for t in range(DT):
                eng.wait_ge(squared, t + 1)
                mm = eng.matmul(ps[:, :], k.ones, sq[:, t, :], start=(t == 0), stop=(t == DT - 1))
            mm.then_inc(added, 1)

        @block.scalar
        def _(eng):
            for t in range(DT):
                eng.activation(sq[:, t, :], k.x[:, t, :], ACT.Square).then_inc(squared, 1)
            eng.wait_ge(added, 1)
            eng.activation(rstd[:, :], ps[:, :], ACT.Ln, scale=1.0 / D, bias=k.eps[:, 0:1]).then_inc(logged, 1)
            eng.wait_ge(logged, 1)
            eng.activation(rstd[:, :], rstd[:, :], ACT.Exp, scale=-0.5).then_inc(inv_ready, 1)

        @block.vector
        def _(eng):
            eng.wait_ge(inv_ready, 1)
            for t in range(DT):
                eng.scalar_tensor_tensor(out=k.x[:, t, :], in0=k.x[:, t, :], scalar=gain[:, t:t + 1], in1=rstd[:, :],
                                         op0=ALU.mult, op1=ALU.mult).then_inc(scaled, 1)


class Slot:

    def __init__(self, loads, nk, tiles, rhs, k0, first, last, kind, index):
        self.loads, self.nk, self.tiles, self.rhs, self.k0 = loads, nk, tiles, rhs, k0
        self.first, self.last, self.kind, self.index = first, last, kind, index


class Norm:
    SEMS = 8

    def __init__(self, nc, k, ctx, name, sems, gain, shift, hi, lo, sq, part, h):
        (self.squared, self.added, self.logged, self.inv_ready, self.scaled, self.h_ready, self.hi_ready,
         self.lo_ready) = sems
        self.k, self.gain, self.shift, self.hi, self.lo = k, gain, shift, hi, lo
        self.sq, self.part, self.h = sq, part, h
        self.rstd = ctx.enter_context(nc.sbuf_tensor(f"{name}_rstd", [P, S], F32))
        self.ps = ctx.enter_context(nc.psum_tensor(f"{name}_psn", [P, 512], F32))

    def square(self, eng):
        for t in range(DT):
            if t >= 2:
                eng.wait_ge(self.added, t - 1)
            eng.activation(self.sq[:, t % 2, :], self.k.x[:, t, :], ACT.Square).then_inc(self.squared, 1)

    def add(self, eng):
        for t in range(DT):
            eng.wait_ge(self.squared, t + 1)
            eng.matmul(self.ps[:, :], self.k.ones, self.sq[:, t % 2, :], start=(t == 0), stop=(t == DT - 1))\
               .then_inc(self.added, 1)

    def invert(self, eng):
        eng.wait_ge(self.added, DT)
        eng.activation(self.rstd[:, :], self.ps[:, :], ACT.Ln, scale=1.0 / D, bias=self.k.eps[:, 0:1])\
           .then_inc(self.logged, 1)
        eng.wait_ge(self.logged, 1)
        eng.activation(self.rstd[:, :], self.rstd[:, :], ACT.Exp, scale=-0.5).then_inc(self.inv_ready, 1)

    def scale(self, eng, t):
        eng.wait_ge(self.inv_ready, 1)
        if t >= 2:
            eng.wait_ge(self.lo_ready, t - 1)
        out = self.h if self.shift is None else self.part
        ins = eng.scalar_tensor_tensor(out=out[:, t % 2, :], in0=self.k.x[:, t, :], scalar=self.gain[:, t:t + 1],
                                       in1=self.rstd[:, :], op0=ALU.mult, op1=ALU.mult)
        if self.shift is None:
            ins.then_inc(self.h_ready, 1)
        else:
            ins.then_inc(self.scaled, 1)
            eng.wait_ge(self.scaled, t + 1)
            eng.tensor_scalar(self.h[:, t % 2, :], self.part[:, t % 2, :], self.shift[:, t:t + 1], None, ALU.add)\
               .then_inc(self.h_ready, 1)

    def round_hi(self, eng, t):
        eng.wait_ge(self.h_ready, t + 1)
        eng.activation(self.hi[:, t, :], self.h[:, t % 2, :], ACT.Copy).then_inc(self.hi_ready, 1)

    def take_lo(self, eng, t):
        eng.wait_ge(self.hi_ready, t + 1)
        eng.tensor_tensor(self.lo[:, t, :], self.h[:, t % 2, :], self.hi[:, t, :].bitcast(F32), ALU.subtract)\
           .then_inc(self.lo_ready, 1)


def products(nc, k, ph, name, slots, operands, more, need, epilogue, norm=None, side=None):
    RAW, SPLIT = 2, 3
    n_norm, n_side = (Norm.SEMS if norm else 0), (Side.SEMS if side else 0)
    sems = ph.open(4 + RAW + more + n_norm + n_side)
    hi_ready, lo_ready, slot_done, banks_free = sems[:4]
    landed, own, rest = sems[4:4 + RAW], sems[4 + RAW:4 + RAW + more], sems[4 + RAW + more:]
    groups = [s for s in slots if s.last]
    ends = [i + 1 for i, s in enumerate(slots) if s.last]

    def wait_group(eng, g):
        eng.wait_ge(slot_done, ends[g])

    with ExitStack() as ctx:
        raw = ctx.enter_context(nc.sbuf_tensor(f"{name}_raw", [P, RAW, KC, MC], F32))
        w_hi = ctx.enter_context(nc.sbuf_tensor(f"{name}_whi", [P, SPLIT, KC, MC], F32R))
        w_lo = ctx.enter_context(nc.sbuf_tensor(f"{name}_wlo", [P, SPLIT, KC, MC], F32R))
        ps = [[ctx.enter_context(nc.psum_tensor(f"{name}_ps{a}{b}", [P, 512], F32)) for b in (0, 1)] for a in (0, 1)]
        act_epi, vec_epi, pool_epi, buffers = epilogue(ctx, own, wait_group, banks_free, lambda g: ps[g % 2])
        if norm:
            hi, lo = operands["h"]
            norm = Norm(nc, k, ctx, name, rest[:n_norm], *norm, hi, lo, *buffers)
        if side:
            side = Side(nc, k, ctx, f"{name}_ada", rest[n_norm:], *side)
        n_tiles = len(side.tiles) if side else 0

        def beside(i):
            return range(i * n_tiles // len(slots), (i + 1) * n_tiles // len(slots)) if 0 <= i < len(slots) else ()

        block = ctx.enter_context(nc.Block())

        def width(s):
            return max(c + w for c, w in s.tiles)

        @block.sync
        def _(eng):
            for i, s in enumerate(slots):
                if i >= RAW:
                    eng.wait_ge(lo_ready, i - RAW + 1)
                for at, src, w in s.loads:
                    eng.dma_start(raw[:, i % RAW, 0:s.nk, at:at + w], src).then_inc(landed[i % RAW], 16)
                for t in beside(i - SPLIT):
                    side.load(eng, t)
            for i in range(len(slots), len(slots) + SPLIT):
                for t in beside(i - SPLIT):
                    side.load(eng, t)

        arrivals, seen = [], [0] * RAW
        for i, s in enumerate(slots):
            seen[i % RAW] += 16 * len(s.loads)
            arrivals.append(seen[i % RAW])

        @block.scalar
        def _(eng):
            def round_hi(i):
                s = slots[i]
                eng.wait_ge(landed[i % RAW], arrivals[i])
                if i >= SPLIT:
                    eng.wait_ge(slot_done, i - SPLIT + 1)
                eng.activation(w_hi[:, i % SPLIT, 0:s.nk, 0:width(s)], raw[:, i % RAW, 0:s.nk, 0:width(s)], ACT.Copy)\
                   .then_inc(hi_ready, 1)

            if norm:
                norm.square(eng)
                round_hi(0)
                norm.invert(eng)
                for t in range(DT):
                    norm.round_hi(eng, t)
                    if t in (1, 4):
                        round_hi(1 if t == 1 else 2)
            else:
                for i in range(min(SPLIT, len(slots))):
                    round_hi(i)
            g = 0
            for i, s in enumerate(slots):
                if s.last:
                    act_epi(eng, g, s, 0)
                if i + SPLIT < len(slots):
                    round_hi(i + SPLIT)
                if s.last:
                    act_epi(eng, g, s, 1)
                    g += 1

        @block.gpsimd
        def _(eng):
            ph.clear(eng)
            if norm:
                for t in range(DT):
                    norm.take_lo(eng, t)
            for g, s in enumerate(groups):
                pool_epi(eng, g, s)

        @block.vector
        def _(eng):
            def take_lo(i):
                s = slots[i]
                eng.wait_ge(hi_ready, i + 1)
                if i >= SPLIT:
                    eng.wait_ge(slot_done, i - SPLIT + 1)
                eng.tensor_tensor(w_lo[:, i % SPLIT, 0:s.nk, 0:width(s)], raw[:, i % RAW, 0:s.nk, 0:width(s)],
                                  w_hi[:, i % SPLIT, 0:s.nk, 0:width(s)].bitcast(F32), ALU.subtract)\
                   .then_inc(lo_ready, 1)

            if norm:
                take_lo(0)
                for t in range(DT):
                    norm.scale(eng, t)
                    if t in (2, 5):
                        take_lo(1 if t == 2 else 2)
            else:
                for i in range(min(SPLIT, len(slots))):
                    take_lo(i)
            g = banks = 0
            for i, s in enumerate(slots):
                if s.last:
                    vec_epi(eng, g, s)
                    g += 1
                if i + SPLIT < len(slots):
                    take_lo(i + SPLIT)
                for t in beside(i):
                    side.sum(eng, t)
                while side and 4 * banks + 4 <= (beside(i - 3).stop if i >= 3 else 0):
                    side.take(eng, banks)
                    banks += 1
            while side and 4 * banks < n_tiles:
                side.take(eng, banks)
                banks += 1

        @block.tensor
        def _(eng):
            if norm:
                norm.add(eng)
            g = 0
            for i, s in enumerate(slots):
                for t in beside(i - 2):
                    side.turn(eng, t)
                if s.first and g >= 2:
                    eng.wait_ge(banks_free, g - 1)
                eng.wait_ge(lo_ready, i + 1)
                hi, lo = operands[s.rhs]
                for q in range(s.nk):
                    a = s.k0 + q
                    need(eng, own, s, q)
                    if norm and i == 0:
                        eng.wait_ge(norm.lo_ready, q + 1)
                    for b, (c, w) in enumerate(s.tiles):
                        out = ps[g % 2][b][0:w, :]
                        wh, wl = w_hi[:, i % SPLIT, q, c:c + w], w_lo[:, i % SPLIT, q, c:c + w]
                        eng.matmul(out, wh, hi[:, a, :], start=(s.first and q == 0), stop=False)
                        eng.matmul(out, wh, lo[:, a, :], start=False, stop=False)
                        mm = eng.matmul(out, wl, hi[:, a, :], start=False, stop=(s.last and q == s.nk - 1))
                mm.then_inc(slot_done, 1)
                g += s.last
            for i in (len(slots) - 2, len(slots) - 1):
                for t in beside(i):
                    side.turn(eng, t)


def weights(w, l, col, width, k0, nk):
    return w[bass.ds(l, 1), k0 * P:(k0 + nk) * P, col:col + width].rearrange("a (q p) n -> p (a q) n", p=P)


def feed_forward(nc, k, ph, name, l, w_in, w_out, hidden, per_round, gated, norm, gate_col, side=None):
    slots = []
    n_hidden = hidden // P
    for r0 in range(0, n_hidden, per_round):
        if gated:
            for j in range(r0, r0 + per_round):
                slots.append(Slot([(0, weights(w_in, l, j * P, P, 0, DT), P),
                                   (P, weights(w_in, l, hidden + j * P, P, 0, DT), P)],
                                  DT, [(0, P), (P, P)], "h", 0, True, True, "in", j - r0))
        else:
            for j in range(r0, r0 + per_round, 2):
                slots.append(Slot([(0, weights(w_in, l, j * P, MC, 0, DT), MC)], DT, [(0, P), (P, P)], "h", 0,
                                  True, True, "in", j - r0))
        for m in range(0, DT, 2):
            parts = -(-per_round // KC)
            for part in range(parts):
                q = part * per_round // parts
                nk = (part + 1) * per_round // parts - q
                slots.append(Slot([(0, weights(w_out, l, m * P, MC, r0 + q, nk), MC)], nk, [(0, P), (P, P)], "g", q,
                                  q == 0, q + nk == per_round, "out", m))
    tiles = 1 if gated else 2
    before = {id(s): i // (len(slots) * per_round // n_hidden) * per_round for i, s in enumerate(slots)}
    n_in, ins = 0, []
    for s in slots:
        if s.last:
            ins.append(n_in)
            n_in += s.kind == "in"

    with ExitStack() as ctx:
        g_hi = ctx.enter_context(nc.sbuf_tensor(f"{name}_ghi", [P, per_round, S], F32R))
        g_lo = ctx.enter_context(nc.sbuf_tensor(f"{name}_glo", [P, per_round, S], F32R))
        hi, lo = (ctx.enter_context(nc.sbuf_tensor(f"{name}_h{part}", [P, DT, S], F32R)) for part in ("hi", "lo"))

        def epilogue(ctx, own, wait_group, banks_free, banks):
            t_ready, u_ready, v_ready, ghi_ready, glo_ready = own
            t = ctx.enter_context(nc.sbuf_tensor(f"{name}_t", [P, 2, tiles, S], F32))
            u = ctx.enter_context(nc.sbuf_tensor(f"{name}_u", [P, 2, S], F32))
            v = ctx.enter_context(nc.sbuf_tensor(f"{name}_v", [P, 2, tiles, S], F32))

            def act_epi(eng, g, s, part):
                n = ins[g]
                if s.kind == "out":
                    return
                if part == 0:
                    wait_group(eng, g)
                    if n >= 2:
                        eng.wait_ge(v_ready, tiles * (n - 1))
                    if gated:
                        eng.activation(t[:, n % 2, 0, :], banks(g)[0][:, :], ACT.Tanh, scale=0.5).then_inc(t_ready, 1)
                    else:
                        for b in (0, 1):
                            eng.activation(t[:, n % 2, b, :], banks(g)[b][:, :], ACT.Relu).then_inc(t_ready, 1)
                else:
                    for b in range(tiles):
                        eng.wait_ge(v_ready, tiles * n + b + 1)
                        eng.activation(g_hi[:, s.index + b, :], v[:, n % 2, b, :], ACT.Copy).then_inc(ghi_ready, 1)

            def pool_epi(eng, g, s):
                if s.kind == "out":
                    return
                n = ins[g]
                for b in range(tiles):
                    eng.wait_ge(ghi_ready, tiles * n + b + 1)
                    eng.tensor_tensor(g_lo[:, s.index + b, :], v[:, n % 2, b, :], g_hi[:, s.index + b, :].bitcast(F32),
                                      ALU.subtract).then_inc(glo_ready, 1)

            def vec_epi(eng, g, s):
                n = ins[g]
                if s.kind == "out":
                    wait_group(eng, g)
                    for b in (0, 1):
                        m = s.index + b
                        if gate_col is None:
                            ins_ = eng.tensor_tensor(k.x[:, m, :], banks(g)[b][:, :], k.x[:, m, :], ALU.add)
                        else:
                            ins_ = eng.scalar_tensor_tensor(out=k.x[:, m, :], in0=banks(g)[b][:, :],
                                                            scalar=gate_col[:, m:m + 1], in1=k.x[:, m, :],
                                                            op0=ALU.mult, op1=ALU.add)
                    ins_.then_inc(banks_free, 1)
                    eng.wait_ge(banks_free, g + 1)
                    return
                eng.wait_ge(t_ready, tiles * (n + 1))
                if n >= 2:
                    eng.wait_ge(glo_ready, tiles * (n - 1))
                if gated:
                    eng.scalar_tensor_tensor(out=u[:, 0, :], in0=t[:, n % 2, 0, :], scalar=1.0, in1=banks(g)[0][:, :],
                                             op0=ALU.add, op1=ALU.mult).then_inc(u_ready, 1)
                    eng.wait_ge(u_ready, n + 1)
                    eng.scalar_tensor_tensor(out=v[:, n % 2, 0, :], in0=u[:, 0, :], scalar=0.5, in1=banks(g)[1][:, :],
                                             op0=ALU.mult, op1=ALU.mult).then_inc(v_ready, 1)
                else:
                    for b in (0, 1):
                        eng.tensor_tensor(v[:, n % 2, b, :], t[:, n % 2, b, :], t[:, n % 2, b, :], ALU.mult)\
                           .then_inc(v_ready, 1)
                eng.wait_ge(v_ready, tiles * (n + 1))
                eng.sem_inc(banks_free, 1)

            return act_epi, vec_epi, pool_epi, (t[:, :, 0, :], u, v[:, :, 0, :])

        def need(eng, own, s, q):
            if s.kind == "out" and s.index == 0:
                eng.wait_ge(own[4], before[id(s)] + s.k0 + q + 1)

        products(nc, k, ph, name, slots, {"h": (hi, lo), "g": (g_hi, g_lo)}, 5, need, epilogue,
                 norm, side)


def project(nc, k, ph, name, l, w, tiles, hi, lo, store, norm=None, room=None):
    slots = []
    i = 0
    while i < len(tiles):
        col, wid = tiles[i]
        if i + 1 < len(tiles) and tiles[i + 1][0] == col + wid and wid == P:
            two = wid + tiles[i + 1][1]
            slots.append(Slot([(0, weights(w, l, col, two, 0, DT), two)], DT, [(0, P), (P, two - P)], "h", 0,
                              True, True, "in", i))
            i += 2
        else:
            slots.append(Slot([(0, weights(w, l, col, wid, 0, DT), wid)], DT, [(0, wid)], "h", 0, True, True, "in", i))
            i += 1

    def epilogue(ctx, own, wait_group, banks_free, banks):
        def nothing(eng, g, s, *part):
            return

        def vec_epi(eng, g, s):
            wait_group(eng, g)
            for b, (c, wid) in enumerate(s.tiles):
                ins = store(eng, s.index + b, banks(g)[b][0:wid, :])
            ins.then_inc(banks_free, 1)

        return nothing, vec_epi, nothing, [room[:, 2 * i:2 * i + 2, :] for i in range(3)] if norm else ()

    products(nc, k, ph, name, slots, {"h": (hi, lo)}, 0, lambda eng, own, s, q: None, epilogue, norm)


def split(nc, k, ph, src, hi, lo, n):
    hi_ready, lo_ready = ph.open(2)
    with nc.Block() as block:
        @block.scalar
        def _(eng):
            for t in range(n):
                eng.activation(hi[:, t, :], src[:, t, :], ACT.Copy).then_inc(hi_ready, 1)

        @block.gpsimd
        def _(eng):
            ph.clear(eng)
            for t in range(n):
                eng.wait_ge(hi_ready, t + 1)
                eng.tensor_tensor(lo[:, t, :], src[:, t, :], hi[:, t, :].bitcast(F32), ALU.subtract)\
                   .then_inc(lo_ready, 1)


def finish(nc, k, ph, out):
    turned, copied, stored = ph.open(3)
    with ExitStack() as ctx:
        y = ctx.enter_context(nc.sbuf_tensor("y_rows", [P, 4, D], F32))
        ps = [ctx.enter_context(nc.psum_tensor(f"ps_fin{i}", [P, 512], F32)) for i in (0, 1)]
        block = ctx.enter_context(nc.Block())

        @block.gpsimd
        def _(eng):
            ph.clear(eng)

        @block.tensor
        def _(eng):
            for i in range(8):
                if i >= 2:
                    eng.wait_ge(copied, i - 1)
                t, half = i // 2, i % 2
                for j in range(4):
                    mm = eng.transpose(ps[i % 2][:, j * P:(j + 1) * P], k.x[:, 4 * half + j, t * P:(t + 1) * P], k.ident)
                mm.then_inc(turned, 1)

        @block.vector
        def _(eng):
            for i in range(8):
                eng.wait_ge(turned, i + 1)
                eng.tensor_copy(y[:, i // 2, (i % 2) * 512:(i % 2 + 1) * 512], ps[i % 2][:, :]).then_inc(copied, 1)

        @block.sync
        def _(eng):
            rows = out.rearrange("b (t p) d -> t p (b d)", p=P)
            for t in range(4):
                eng.wait_ge(copied, 2 * t + 2)
                eng.dma_start(rows[t], y[:, t, :]).then_inc(stored, 16)
            eng.wait_ge(stored, 64)


def over_heads(ap, n):
    return ap.unsqueeze(1).to_broadcast([ap.shape[0], n, ap.shape[-1]])


def norm_features(nc, k, ph, name, src, groups, sums, eps, gain, dst, mean=False, bias=None, gate=None):
    n = sum(len(tiles) for tiles, _ in groups)
    (mean_ready, centred, squared, summed, logged, inv_ready, scaled, normed, gate_ready, gated, stepped) = ph.open(11)
    with ExitStack() as ctx:
        def sb(nm, shape):
            return ctx.enter_context(nc.sbuf_tensor(f"{name}_{nm}", shape, F32))

        sq = sb("sq", [P, n, S])
        rstd = sb("rstd", [P, len(groups), S])
        cen = sb("cen", [P, n, S]) if mean else None
        th = sb("th", [P, n, S]) if gate is not None else None
        ps_mean = [ctx.enter_context(nc.psum_tensor(f"{name}_psm{i}", [P, 512], F32)) for i in range(2 if mean else 0)]
        ps_sq = [ctx.enter_context(nc.psum_tensor(f"{name}_pss{i}", [P, 512], F32)) for i in (0, 1)]
        block = ctx.enter_context(nc.Block())
        base = cen[:, :, :] if mean else src

        @block.gpsimd
        def _(eng):
            ph.clear(eng)

        @block.tensor
        def _(eng):
            if mean:
                for g, (tiles, _) in enumerate(groups):
                    if g >= 2:
                        eng.wait_ge(centred, g - 1)
                    eng.matmul(ps_mean[g % 2][:, :], sums, src[:, tiles[0], :], start=True, stop=True)\
                       .then_inc(mean_ready, 1)
            done = 0
            for g, (tiles, _) in enumerate(groups):
                if g >= 2:
                    eng.wait_ge(logged, g - 1)
                for t in tiles:
                    eng.wait_ge(squared, done + 1)
                    mm = eng.matmul(ps_sq[g % 2][:, :], sums, sq[:, t, :], start=(t == tiles[0]), stop=(t == tiles[-1]))
                    done += 1
                mm.then_inc(summed, 1)

        @block.scalar
        def _(eng):
            for t in range(n):
                if mean:
                    eng.wait_ge(centred, t + 1)
                eng.activation(sq[:, t, :], base[:, t, :], ACT.Square).then_inc(squared, 1)
            for g, (tiles, count) in enumerate(groups):
                eng.wait_ge(summed, g + 1)
                eng.activation(rstd[:, g, :], ps_sq[g % 2][:, :], ACT.Ln, scale=1.0 / count, bias=eps).then_inc(logged, 1)
            for g in range(len(groups)):
                eng.wait_ge(logged, len(groups))
                eng.activation(rstd[:, g, :], rstd[:, g, :], ACT.Exp, scale=-0.5).then_inc(inv_ready, 1)
            if gate is not None:
                for t in range(n):
                    eng.activation(th[:, t, :], gate[:, t, :], ACT.Tanh, scale=0.5).then_inc(gate_ready, 1)

        @block.vector
        def _(eng):
            if mean:
                for g, (tiles, count) in enumerate(groups):
                    eng.wait_ge(mean_ready, g + 1)
                    eng.scalar_tensor_tensor(out=cen[:, tiles[0], :], in0=ps_mean[g % 2][:, :], scalar=-1.0 / count,
                                             in1=src[:, tiles[0], :], op0=ALU.mult, op1=ALU.add).then_inc(centred, 1)
                eng.wait_ge(centred, len(groups))
            for g, (tiles, _) in enumerate(groups):
                eng.wait_ge(inv_ready, g + 1)
                for t in tiles:
                    eng.scalar_tensor_tensor(out=dst[:, t, :], in0=base[:, t, :], scalar=gain[:, t:t + 1],
                                             in1=rstd[:, g, :], op0=ALU.mult, op1=ALU.mult).then_inc(normed, 1)
            if bias is not None:
                eng.wait_ge(normed, n)
                for t in range(n):
                    eng.tensor_scalar(dst[:, t, :], dst[:, t, :], bias[:, t:t + 1], None, ALU.add).then_inc(scaled, 1)
            if gate is not None:
                eng.wait_ge(normed, n)
                for t in range(n):
                    eng.wait_ge(gate_ready, t + 1)
                    eng.scalar_tensor_tensor(out=th[:, t, :], in0=th[:, t, :], scalar=1.0, in1=gate[:, t, :],
                                             op0=ALU.add, op1=ALU.mult).then_inc(gated, 1)
                    eng.wait_ge(gated, t + 1)
                    eng.scalar_tensor_tensor(out=dst[:, t, :], in0=th[:, t, :], scalar=0.5, in1=dst[:, t, :],
                                             op0=ALU.mult, op1=ALU.mult).then_inc(stepped, 1)


def retention(nc, k, ph, l, z, o):
    W = 2 * S - P
    with ExitStack() as outer:
        def sb(name, shape, dt=F32):
            return outer.enter_context(nc.sbuf_tensor(f"ret_{name}", shape, dt))

        qk = sb("qk", [P, 4, S])
        v = sb("v", [P, 4, 256])
        decay = sb("decay", [P, RET_HEADS, W])
        y = sb("y", [P, 2, S])

        (rated, turned, vturned, cos_done, sin_done, qk_done, vcopied, dist, dist_f, expo, neg, emade) = ph.open(12)
        with ExitStack() as ctx:
            def sb(name, shape, dt=F32):
                return ctx.enter_context(nc.sbuf_tensor(f"ret_{name}", shape, dt))

            rate = sb("rate", [P, 8])
            di = sb("di", [P, W], I32)
            df = sb("df", [P, W])
            dp = sb("dp", [P, 2, W])
            part = sb("part", [P, 2, 2, S])
            ps = [ctx.enter_context(nc.psum_tensor(f"ret_rot{i}", [P, 512], F32)) for i in range(4)]
            pv = [ctx.enter_context(nc.psum_tensor(f"ret_pv{i}", [P, 512], F32)) for i in range(2)]
            block = ctx.enter_context(nc.Block())

            @block.sync
            def _(eng):
                src = k.inp["ret_log_rate"][bass.ds(l, 1), :, :].rearrange("a d h -> a (d h)")
                eng.dma_start(rate[:, :], bcast_rows(src, P)).then_inc(rated, 16)

            @block.gpsimd
            def _(eng):
                ph.clear(eng)
                eng.iota(di[:, :], pattern=[[1, W]], base=-(S - P), channel_multiplier=-1).then_inc(dist, 1)
                eng.wait_ge(dist, 1)
                eng.tensor_copy(df[:, :], di[:, :]).then_inc(dist_f, 1)

            @block.tensor
            def _(eng):
                for t in range(4):
                    eng.matmul(ps[t][:, :], k.rot64, z[:, t, :], start=True, stop=True).then_inc(turned, 1)
                for t in range(2):
                    for j in range(4):
                        mm = eng.transpose(pv[t][:, j * P:(j + 1) * P], z[:, 4 + t, j * P:(j + 1) * P], k.ident)
                    mm.then_inc(vturned, 1)

            @block.scalar
            def _(eng):
                eng.wait_ge(rated, 16)
                eng.activation(rate[:, :], rate[:, :], ACT.Exp).then_inc(neg, 1)
                for t in range(2):
                    eng.wait_ge(vturned, t + 1)
                    eng.activation(v[:, :, t * P:(t + 1) * P], pv[t][:, :].rearrange("p (j f) -> p j f", j=4), ACT.Copy)\
                       .then_inc(vcopied, 1)
                for h in range(RET_HEADS):
                    eng.wait_ge(expo, 2 * h + 2)
                    eng.activation(decay[:, h, :], decay[:, h, :], ACT.Exp, scale=-1.0).then_inc(emade, 1)

            @block.vector
            def _(eng):
                for t in range(4):
                    scale = 1.0 if t < 2 else HD ** -0.5
                    eng.wait_ge(turned, t + 1)
                    if t >= 2:
                        eng.wait_ge(qk_done, t - 1)
                    eng.scalar_tensor_tensor(out=part[:, t % 2, 0, :], in0=ps[t][:, :], scalar=scale, in1=k.sin[:, 1, :],
                                             op0=ALU.mult, op1=ALU.mult).then_inc(sin_done, 1)
                    eng.scalar_tensor_tensor(out=part[:, t % 2, 1, :], in0=z[:, t, :], scalar=scale, in1=k.cos[:, 1, :],
                                             op0=ALU.mult, op1=ALU.mult).then_inc(cos_done, 1)
                    eng.wait_ge(cos_done, t + 1)
                    eng.tensor_tensor(qk[:, t, :], part[:, t % 2, 0, :], part[:, t % 2, 1, :], ALU.add)\
                       .then_inc(qk_done, 1)
                eng.wait_ge(dist_f, 1)
                eng.tensor_scalar(dp[:, 0, :], df[:, :], 0.0, None, ALU.max)
                eng.tensor_scalar(dp[:, 1, :], df[:, :], -1.0, 0.0, ALU.mult, ALU.max).then_inc(sin_done, 1)
                eng.wait_ge(sin_done, 5)
                eng.wait_ge(neg, 1)
                for h in range(RET_HEADS):
                    eng.tensor_scalar(decay[:, h, :], dp[:, 0, :], rate[:, h:h + 1], None, ALU.mult).then_inc(expo, 1)
                    eng.wait_ge(expo, 2 * h + 1)
                    eng.scalar_tensor_tensor(out=decay[:, h, :], in0=dp[:, 1, :], scalar=rate[:, 4 + h:5 + h],
                                             in1=decay[:, h, :], op0=ALU.mult, op1=ALU.add).then_inc(expo, 1)

        scored, weighed, summed, copied = ph.open(4)
        with ExitStack() as ctx:
            prob = ctx.enter_context(nc.sbuf_tensor("ret_prob", [P, 3, S], F32))
            ps = [ctx.enter_context(nc.psum_tensor(f"ret_ps{i}", [P, 512], F32)) for i in range(3)]
            po = [ctx.enter_context(nc.psum_tensor(f"ret_po{i}", [P, 512], F32)) for i in range(2)]
            block = ctx.enter_context(nc.Block())
            units = [(h, j) for h in range(RET_HEADS) for j in range(4)]

            @block.gpsimd
            def _(eng):
                ph.clear(eng)

            @block.tensor
            def _(eng):
                def scores(u):
                    h, j = units[u]
                    r = slice(64 * (h % 2), 64 * (h % 2) + 64)
                    if u >= 3:
                        eng.wait_ge(weighed, u - 2)
                    eng.matmul(ps[u % 3][:, :], qk[r, 2 + h // 2, j * P:(j + 1) * P], qk[r, h // 2, :],
                               start=True, stop=True).then_inc(scored, 1)

                scores(0)
                scores(1)
                for u, (h, j) in enumerate(units):
                    if u + 2 < len(units):
                        scores(u + 2)
                    r = slice(64 * (h % 2), 64 * (h % 2) + 64)
                    eng.wait_ge(weighed, u + 1)
                    eng.matmul(po[h // 2][r, :], v[:, j, h * 64:(h + 1) * 64], prob[:, u % 3, :],
                               start=(j == 0), stop=(j == 3)).then_inc(summed, 1)

            @block.vector
            def _(eng):
                for u, (h, j) in enumerate(units):
                    eng.wait_ge(scored, u + 1)
                    if u >= 3:
                        eng.wait_ge(summed, u - 2)
                    at = S - P - j * P
                    eng.tensor_tensor(prob[:, u % 3, :], ps[u % 3][:, :], decay[:, h, at:at + S], ALU.mult)\
                       .then_inc(weighed, 1)

            @block.scalar
            def _(eng):
                for t in range(2):
                    eng.wait_ge(summed, 8 * (t + 1))
                    eng.activation(y[:, t, :], po[t][:, :], ACT.Copy).then_inc(copied, 1)

        at = AT_1["ret_gn_g"]
        norm_features(nc, k, ph, "retn", y[:, :, :], [([0], HD), ([1], HD)], k.sum64, k.eps[:, 2:3],
                      k.vec1[:, at:at + 2], o, mean=True, gate=z[:, 6:8, :])


def latent_attention(nc, k, ph, l, z, kpe, o):
    SCALE = float(MLA_QK) ** -0.5
    with ExitStack() as outer:
        def sb(name, shape, dt=F32):
            return outer.enter_context(nc.sbuf_tensor(f"mla_{name}", shape, dt))

        w_q = sb("wq", [P, 3, MLA_HEADS * MLA_QK])
        w_kv = sb("wkv", [P, 2, MLA_HEADS * P])
        v = sb("v", [P, 4, MLA_HEADS * MLA_V])
        key = sb("key", [MLA_QK, 2, S])
        at = AT_1["mla_q_norm_g"]
        norm_features(nc, k, ph, "mlan", z, [([0, 1, 2], MLA_Q), ([3, 4], MLA_KV)], k.ones, k.eps[:, 0:1],
                      k.vec1[:, at:at + 5], z)

        loaded, vmade, vcopied, put, cos_done, key_done = ph.open(6)
        with ExitStack() as ctx:
            part = ctx.enter_context(nc.sbuf_tensor("mla_kpart", [MLA_QK, 2, S], F32))
            ps = [ctx.enter_context(nc.psum_tensor(f"mla_pv{i}", [P, 512], F32)) for i in range(2)]
            pk = [ctx.enter_context(nc.psum_tensor(f"mla_pk{i}", [P, 512], F32)) for i in range(2)]
            block = ctx.enter_context(nc.Block())

            @block.sync
            def _(eng):
                eng.dma_start(w_kv[:, :, :], weights(k.inp["mla_w_ukv"], l, 0, MLA_HEADS * P, 0, 2)).then_inc(loaded, 16)
                eng.dma_start(w_q[:, :, :], weights(k.inp["mla_w_uq"], l, 0, MLA_HEADS * MLA_QK, 0, 3)).then_inc(loaded, 16)

            @block.gpsimd
            def _(eng):
                ph.clear(eng)

            @block.tensor
            def _(eng):
                eng.matmul(pk[0][0:MLA_QK, :], k.put32, kpe, start=True, stop=True).then_inc(put, 1)
                eng.matmul(pk[1][0:MLA_QK, :], k.putrot32, kpe, start=True, stop=True).then_inc(put, 1)
                eng.wait_ge(loaded, 32)
                for i in range(4):
                    if i >= 2:
                        eng.wait_ge(vcopied, i - 1)
                    for q in range(2):
                        wv = w_kv[:, q, :].rearrange("p (h c) -> p h c", c=P)[:, :, MLA_NOPE:P]
                        mm = eng.matmul(ps[i % 2][:, :], z[:, 3 + q, i * P:(i + 1) * P], wv, start=(q == 0), stop=(q == 1))
                    mm.then_inc(vmade, 1)

            @block.scalar
            def _(eng):
                for i in range(4):
                    eng.wait_ge(vmade, i + 1)
                    eng.activation(v[:, i, :], ps[i % 2][:, :], ACT.Copy).then_inc(vcopied, 1)

            @block.vector
            def _(eng):
                eng.wait_ge(put, 2)
                eng.tensor_tensor(part[:, 0, :], pk[0][0:MLA_QK, :], k.cos[0:MLA_QK, 0, :], ALU.mult).then_inc(cos_done, 1)
                eng.tensor_tensor(part[:, 1, :], pk[1][0:MLA_QK, :], k.sin[0:MLA_QK, 0, :], ALU.mult).then_inc(cos_done, 1)
                eng.wait_ge(cos_done, 2)
                for b in (0, 1):
                    eng.tensor_tensor(key[:, b, :], part[:, 0, :], part[:, 1, :], ALU.add).then_inc(key_done, 1)

        (q_made, q_copied, q_rot, k_made, k_copied, q_cos, q_sin, q_ready, scored, maxed, nm_ready, exp_done,
         rr_ready, normed, p_turned, p_copied, o_made, o_copied) = ph.open(18)
        with ExitStack() as ctx:
            def sb(name, shape, dt=F32):
                return ctx.enter_context(nc.sbuf_tensor(f"mla_{name}", shape, dt))

            qs, qa, qb = (sb(n, [MLA_QK, S]) for n in ("qs", "qa", "qb"))
            query = sb("query", [MLA_QK, 2, S])
            m, nm, rs, rr = (sb(n, [P, 4]) for n in ("m", "nm", "rs", "rr"))
            prob = sb("prob", [P, 4, S])
            pt = sb("pt", [P, 2, S])
            pq, pr, pk = (ctx.enter_context(nc.psum_tensor(f"mla_{n}", [P, 512], F32)) for n in ("pq", "pr", "pk2"))
            ps = [ctx.enter_context(nc.psum_tensor(f"mla_ps{i}", [P, 512], F32)) for i in range(2)]
            pp = [ctx.enter_context(nc.psum_tensor(f"mla_pp{i}", [P, 512], F32)) for i in range(2)]
            po = ctx.enter_context(nc.psum_tensor("mla_po", [P, 512], F32))
            block = ctx.enter_context(nc.Block())
            H = MLA_HEADS

            @block.gpsimd
            def _(eng):
                ph.clear(eng)

            @block.tensor
            def _(eng):
                def prepare(h):
                    if h >= 1:
                        eng.wait_ge(q_cos, h)
                        eng.wait_ge(k_copied, h)
                        eng.wait_ge(q_sin, h)
                    for q in range(3):
                        mm = eng.matmul(pq[0:MLA_QK, :], w_q[:, q, h * MLA_QK:(h + 1) * MLA_QK], z[:, q, :],
                                        start=(q == 0), stop=(q == 2))
                    mm.then_inc(q_made, 1)
                    for q in range(2):
                        mm = eng.matmul(pk[0:MLA_NOPE, :], w_kv[:, q, h * P:h * P + MLA_NOPE], z[:, 3 + q, :],
                                        start=(q == 0), stop=(q == 1))
                    mm.then_inc(k_made, 1)
                    eng.wait_ge(q_copied, h + 1)
                    eng.matmul(pr[0:MLA_QK, :], k.rot32, qs[:, :], start=True, stop=True).then_inc(q_rot, 1)

                prepare(0)
                for h in range(H):
                    eng.wait_ge(q_ready, h + 1)
                    eng.wait_ge(k_copied, h + 1)
                    for i in range(4):
                        u = 4 * h + i
                        if u >= 2:
                            eng.wait_ge(exp_done, u - 1)
                        eng.matmul(ps[u % 2][:, :], query[:, h % 2, i * P:(i + 1) * P], key[:, h % 2, :],
                                   start=True, stop=True).then_inc(scored, 1)
                    if h + 1 < H:
                        prepare(h + 1)
                    eng.wait_ge(normed, 4 * (h + 1))
                    r = slice(64 * (h % 2), 64 * (h % 2) + 64)

                    def turn(j):
                        u = 4 * h + j
                        if u >= 2:
                            eng.wait_ge(p_copied, u - 1)
                        for i in range(4):
                            mm = eng.transpose(pp[u % 2][:, i * P:(i + 1) * P], prob[:, i, j * P:(j + 1) * P], k.ident)
                        mm.then_inc(p_turned, 1)

                    turn(0)
                    if h % 2 == 0 and h >= 2:
                        eng.wait_ge(o_copied, h // 2)
                    for j in range(4):
                        if j < 3:
                            turn(j + 1)
                        u = 4 * h + j
                        eng.wait_ge(p_copied, u + 1)
                        eng.matmul(po[r, :], v[:, j, h * 64:(h + 1) * 64], pt[:, u % 2, :], start=(j == 0), stop=(j == 3))\
                           .then_inc(o_made, 1)

            @block.scalar
            def _(eng):
                def prepare(h):
                    eng.wait_ge(q_made, h + 1)
                    if h >= 1:
                        eng.wait_ge(q_rot, h)
                    eng.activation(qs[:, :], pq[0:MLA_QK, :], ACT.Copy).then_inc(q_copied, 1)
                    eng.wait_ge(k_made, h + 1)
                    if h >= 2:
                        eng.wait_ge(scored, 4 * (h - 1))
                    eng.activation(key[0:MLA_NOPE, h % 2, :], pk[0:MLA_NOPE, :], ACT.Copy).then_inc(k_copied, 1)

                prepare(0)
                for h in range(H):
                    for i in range(4):
                        u = 4 * h + i
                        eng.wait_ge(nm_ready, u + 1)
                        if h >= 1 and i == 0:
                            eng.wait_ge(p_turned, 4 * h)
                        eng.activation(prob[:, i, :], ps[u % 2][:, :], ACT.Exp, scale=SCALE, bias=nm[:, i:i + 1],
                                       accum_out=rs[:, i:i + 1]).then_inc(exp_done, 1)
                    if h + 1 < H:
                        prepare(h + 1)
                    for j in range(4):
                        u = 4 * h + j
                        eng.wait_ge(p_turned, u + 1)
                        if u >= 2:
                            eng.wait_ge(o_made, u - 1)
                        eng.activation(pt[:, u % 2, :], pp[u % 2][:, :], ACT.Copy).then_inc(p_copied, 1)

            @block.vector
            def _(eng):
                def rotate(h):
                    eng.wait_ge(q_copied, h + 1)
                    if h >= 1:
                        eng.wait_ge(q_ready, h)
                    eng.tensor_tensor(qa[:, :], qs[:, :], k.cos[0:MLA_QK, 0, :], ALU.mult).then_inc(q_cos, 1)
                    eng.wait_ge(q_rot, h + 1)
                    eng.tensor_tensor(qb[:, :], pr[0:MLA_QK, :], k.sin[0:MLA_QK, 0, :], ALU.mult).then_inc(q_sin, 1)
                    eng.wait_ge(q_sin, h + 1)
                    if h >= 2:
                        eng.wait_ge(scored, 4 * (h - 1))
                    eng.tensor_tensor(query[:, h % 2, :], qa[:, :], qb[:, :], ALU.add).then_inc(q_ready, 1)

                rotate(0)
                for h in range(H):
                    for i in range(4):
                        u = 4 * h + i
                        eng.wait_ge(scored, u + 1)
                        eng.tensor_reduce(m[:, i:i + 1], ps[u % 2][:, :], AX, ALU.max).then_inc(maxed, 1)
                        eng.wait_ge(maxed, u + 1)
                        if h >= 1:
                            eng.wait_ge(exp_done, u - 3)
                        eng.tensor_scalar(nm[:, i:i + 1], m[:, i:i + 1], -SCALE, None, ALU.mult).then_inc(nm_ready, 1)
                    for i in range(4):
                        u = 4 * h + i
                        eng.wait_ge(exp_done, u + 1)
                        eng.reciprocal(rr[:, i:i + 1], rs[:, i:i + 1]).then_inc(rr_ready, 1)
                        eng.wait_ge(rr_ready, u + 1)
                        eng.tensor_scalar(prob[:, i, :], prob[:, i, :], rr[:, i:i + 1], None, ALU.mult).then_inc(normed, 1)
                    if h + 1 < H:
                        rotate(h + 1)
                    if h % 2 == 1:
                        eng.wait_ge(o_made, 4 * (h + 1))
                        eng.tensor_copy(o[:, h // 2, :], po[:, :]).then_inc(o_copied, 1)


def mixers_1(nc, k, ph, l, mod):
    with ExitStack() as outer:
        z_rw = outer.enter_context(nc.sbuf_tensor("z_rw", [P, 9, S + 2], F32))[:, :, :]
        o = outer.enter_context(nc.sbuf_tensor("o_cols", [P, DT, S], F32))
        with ExitStack() as ctx:
            z_mla = ctx.enter_context(nc.sbuf_tensor("z_mla", [P, 5, S], F32))[:, :, :]
            z_kpe = ctx.enter_context(nc.sbuf_tensor("z_kpe", [32, S], F32))[:, :]
            z_ret = ctx.enter_context(nc.sbuf_tensor("z_ret", [P, 8, S], F32))[:, :, :]
            with operand(nc, "mix_h", DT) as (hi, lo):
                ret0 = RW_COLS + MLA_COLS
                tiles = [(t * P, P) for t in range(14)] + [(14 * P, 32)] + [(ret0 + t * P, P) for t in range(8)]

                def store(eng, t, ps):
                    if t < 9:
                        return eng.tensor_copy(z_rw[:, t, 1:S + 1], ps)
                    if t < 14:
                        return eng.tensor_copy(z_mla[:, t - 9, :], ps)
                    if t == 14:
                        return eng.tensor_copy(z_kpe, ps)
                    return eng.tensor_copy(z_ret[:, t - 15, :], ps)

                project(nc, k, ph, "in1", l, k.inp["w_in"], tiles, hi, lo, store, (mod(4), mod(3)), o)
            latent_attention(nc, k, ph, l, z_mla, z_kpe, o[:, 2:6, :])
            retention(nc, k, ph, l, z_ret, o[:, 6:8, :])
        rwkv(nc, k, ph, l, z_rw, o[:, 0:2, :])
        with operand(nc, "o", DT) as (hi, lo):
            split(nc, k, ph, o, hi, lo, DT)
            add_projected(nc, k, ph, "out1", l, k.inp["w_out"], hi, lo, mod(5))


def add_projected(nc, k, ph, name, l, w, hi, lo, gate_col):
    def store(eng, m, ps):
        if gate_col is None:
            return eng.tensor_tensor(k.x[:, m, :], ps, k.x[:, m, :], ALU.add)
        return eng.scalar_tensor_tensor(out=k.x[:, m, :], in0=ps, scalar=gate_col[:, m:m + 1], in1=k.x[:, m, :],
                                        op0=ALU.mult, op1=ALU.add)

    project(nc, k, ph, name, l, w, [(t * P, P) for t in range(DT)], hi, lo, store)


LEVELS = 5


def rwkv_plan():
    order = []
    for b in range(S // P):
        for d in (0, 1):
            order += [("MT", d, b, 0, "v"), ("M", d, b, 0, "v")]
        for d in (0, 1):
            order += [("AB", d, b, 0, "s"), ("K", d, b, 0, "s")]
        order += [("N", d, b, 0, "v") for d in (0, 1)]
        for lv in range(1, LEVELS + 1):
            for d in (0, 1):
                order.append(("Z", d, b, lv, "s"))
            if lv == 1:
                order += [("G", d, b, 0, "s") for d in (0, 1)]
            if lv == 2:
                order += [("RK", d, b, 0, "v") for d in (0, 1)]
            if lv == 3:
                order += [("RB", d, b, 0, "v") for d in (0, 1)]
            for d in (0, 1):
                if lv < LEVELS:
                    order.append(("X", d, b, lv, "v"))
                order.append(("XT", d, b, lv, "v"))
        for d in (0, 1):
            order.append(("TA", d, b, 0, "s"))
        for d in (0, 1):
            order += [("R", d, b, 0, "v"), ("Y", d, b, 0, "v"), ("W", d, b, 0, "v"), ("Q", d, b, 0, "s")]
    place, reads = {}, {"v": 0, "s": 0}
    for n, (name, d, b, lv, reader) in enumerate(order):
        reads[reader] += 1
        place[name, d, b, lv] = (n, reader, reads[reader])
    return order, place


def rwkv(nc, k, ph, l, z, o):
    E_HALF = 0.6065306597126334
    V = k.vec1

    def cols(name, n):
        return V[:, AT_1[name]:AT_1[name] + n]

    with ExitStack() as outer:
        def sb(name, shape, dt=F32):
            return outer.enter_context(nc.sbuf_tensor(f"rw_{name}", shape, dt))

        gate = sb("gate", [P, 2, S])
        feat = {n: sb(n, [P, 4, S]) for n in ("A", "B", "K", "R")}
        vt = sb("vt", [P, 4, 256])
        rho = sb("rho", [P, 4, NCH])
        carry = sb("carry", [P, 4, NCH])
        with ExitStack() as prep:
            def sb(name, shape, dt=F32):
                return prep.enter_context(nc.sbuf_tensor(f"rw_{name}", shape, dt))

            lw = sb("lw", [P, 4, S])
            a = sb("a", [P, 4, S])
            kk = sb("kk", [P, 2, S])

            (loaded, padded, summed2, diffed, mixed, tanh_done, w_made, w_tanh, w_done, sg_made, sg_done, g_made,
             k_scaled, k_squared, k_summed, k_max, k_root, k_inv, k_done, half) = ph.open(20)
            with ExitStack() as ctx:
                def sb(name, shape, dt=F32):
                    return ctx.enter_context(nc.sbuf_tensor(f"rw_{name}", shape, dt))

                w_up, a_up, g_up = sb("w_up", [P, 256]), sb("a_up", [P, 256]), sb("g_up", [P, 256])
                nb = sb("nb", [P, 9, S])
                th_w, sg = sb("th_w", [P, S]), sb("sg", [P, S])
                hw = sb("hw", [P, 8])
                kx, sq, kn = sb("kx", [P, 2, S]), sb("sq", [P, 2, S]), sb("kn", [P, 2, S])
                ps = [ctx.enter_context(nc.psum_tensor(f"rw_ps{i}", [P, 512], F32)) for i in range(4)]
                pg = [ctx.enter_context(nc.psum_tensor(f"rw_pg{i}", [P, 512], F32)) for i in range(2)]
                pk = [ctx.enter_context(nc.psum_tensor(f"rw_pk{i}", [P, 512], F32)) for i in range(2)]
                block = ctx.enter_context(nc.Block())
                mid = z[:, :, 1:S + 1]

                @block.sync
                def _(eng):
                    for t, n in ((w_up, "rwkv_w_up"), (a_up, "rwkv_a_up")):
                        eng.dma_start(t[:, :], k.inp[n][bass.ds(l, 1), :, :, :].rearrange("a d r c -> (a d r) c"))\
                           .then_inc(loaded, 16)
                    eng.dma_start(g_up[:, :], k.inp["rwkv_g_up"][bass.ds(l, 1), :, :].rearrange("a r c -> (a r) c"))\
                       .then_inc(loaded, 16)

                @block.gpsimd
                def _(eng):
                    ph.clear(eng)
                    eng.memset(z[:, :, 0:1], 0.0).then_inc(padded, 1)
                    eng.memset(z[:, :, S + 1:S + 2], 0.0).then_inc(padded, 1)

                @block.vector
                def _(eng):
                    eng.wait_ge(padded, 2)
                    eng.tensor_tensor(nb[:, :, :], z[:, :, 0:S], z[:, :, 2:S + 2], ALU.add).then_inc(summed2, 1)
                    eng.wait_ge(summed2, 1)
                    eng.scalar_tensor_tensor(out=nb[:, :, :], in0=nb[:, :, :], scalar=0.5, in1=mid, op0=ALU.mult,
                                             op1=ALU.subtract).then_inc(diffed, 1)
                    eng.tensor_scalar(hw[:, 0:4], cols("rwkv_w0", 4), 0.5, None, ALU.mult).then_inc(half, 1)
                    eng.tensor_scalar(hw[:, 4:8], cols("rwkv_a0", 4), 0.5, None, ALU.mult).then_inc(half, 1)
                    eng.wait_ge(diffed, 1)
                    mu = cols("rwkv_mu", 9)
                    for t in (7, 6, 8, 2, 3, 0, 1, 4, 5):
                        eng.scalar_tensor_tensor(out=z[:, t, 1:S + 1], in0=nb[:, t, :], scalar=mu[:, t:t + 1],
                                                 in1=z[:, t, 1:S + 1], op0=ALU.mult, op1=ALU.add).then_inc(mixed, 1)
                    eng.wait_ge(sg_made, 1)
                    eng.tensor_scalar(sg[:, :], sg[:, :], 0.5, 0.5, ALU.mult, ALU.add).then_inc(sg_done, 1)
                    kkc = cols("rwkv_k_k", 2)
                    for t in (0, 1):
                        eng.wait_ge(mixed, 4 + t)
                        eng.tensor_scalar(kx[:, t, :], z[:, 2 + t, 1:S + 1], kkc[:, t:t + 1], None, ALU.mult)\
                           .then_inc(k_scaled, 1)
                    for t in (0, 1):
                        eng.wait_ge(k_summed, t + 1)
                        eng.tensor_scalar(kn[:, t, :], pk[t][:, :], 1e-24, None, ALU.max).then_inc(k_max, 1)
                    for i in range(8):
                        eng.wait_ge(w_tanh, i + 1)
                        if i < 4:
                            eng.tensor_scalar(lw[:, i, :], lw[:, i, :], -E_HALF / 2, -E_HALF / 2, ALU.mult, ALU.add)\
                               .then_inc(w_done, 1)
                        else:
                            eng.tensor_scalar(a[:, i - 4, :], a[:, i - 4, :], 0.5, 0.5, ALU.mult, ALU.add)\
                               .then_inc(w_done, 1)
                    for t in (0, 1):
                        eng.wait_ge(k_root, t + 1)
                        eng.reciprocal(kn[:, t, :], kn[:, t, :]).then_inc(k_inv, 1)
                        eng.wait_ge(k_inv, t + 1)
                        eng.tensor_tensor(kk[:, t, :], kx[:, t, :], kn[:, t, :], ALU.mult).then_inc(k_done, 1)

                @block.scalar
                def _(eng):
                    eng.wait_ge(mixed, 1)
                    eng.activation(th_w[:, :], z[:, 7, 1:S + 1], ACT.Tanh).then_inc(tanh_done, 1)
                    eng.wait_ge(mixed, 2)
                    eng.activation(sg[:, :], z[:, 6, 1:S + 1], ACT.Tanh, scale=0.5).then_inc(sg_made, 1)
                    for t in (0, 1):
                        eng.wait_ge(k_scaled, t + 1)
                        eng.activation(sq[:, t, :], kx[:, t, :], ACT.Square).then_inc(k_squared, 1)
                    eng.wait_ge(half, 2)
                    for i in range(8):
                        eng.wait_ge(w_made, i + 1)
                        to = lw[:, i, :] if i < 4 else a[:, i - 4, :]
                        eng.activation(to, ps[i % 4][:, :], ACT.Tanh, scale=0.5, bias=hw[:, i:i + 1]).then_inc(w_tanh, 1)
                    for t in (0, 1):
                        eng.wait_ge(g_made, t + 1)
                        eng.activation(gate[:, t, :], pg[t][:, :], ACT.Copy)
                    for t in (0, 1):
                        eng.wait_ge(k_max, t + 1)
                        eng.activation(kn[:, t, :], kn[:, t, :], ACT.Sqrt).then_inc(k_root, 1)

                @block.tensor
                def _(eng):
                    eng.wait_ge(loaded, 48)
                    eng.wait_ge(tanh_done, 1)
                    for i in range(8):
                        if i == 4:
                            eng.wait_ge(mixed, 3)
                        if i >= 4:
                            eng.wait_ge(w_tanh, i - 3)
                        d, t = (i % 4) // 2, i % 2
                        r = slice(64 * d, 64 * d + 64)
                        up, src = (w_up, th_w[r, :]) if i < 4 else (a_up, z[r, 8, 1:S + 1])
                        eng.matmul(ps[i % 4][:, :], up[r, t * P:(t + 1) * P], src, start=True, stop=True)\
                           .then_inc(w_made, 1)
                    for t in (0, 1):
                        eng.wait_ge(k_squared, t + 1)
                        eng.matmul(pk[t][:, :], k.sum64, sq[:, t, :], start=True, stop=True).then_inc(k_summed, 1)
                    eng.wait_ge(sg_done, 1)
                    for t in (0, 1):
                        eng.matmul(pg[t][:, :], g_up[:, t * P:(t + 1) * P], sg[:, :], start=True, stop=True)\
                           .then_inc(g_made, 1)

            (scanned, rho_done, l_ref, l_ex, e_neg, e_ex, e_in, km1, km2, ba_done, f_done, vturned, vcopied, rsum,
             c_done, oka_done) = ph.open(16)
            with ExitStack() as ctx:
                def sb(name, shape, dt=F32):
                    return ctx.enter_context(nc.sbuf_tensor(f"rw_{name}", shape, dt))

                L, Le, En, Ee, km, ba = (sb(n, [P, 2, S]) for n in ("L", "Le", "En", "Ee", "km", "ba"))
                Ep = sb("Ep", [P, 2, S])
                oka = sb("oka", [P, 2])
                ps = [ctx.enter_context(nc.psum_tensor(f"rw_pv{i}", [P, 512], F32)) for i in range(2)]
                block = ctx.enter_context(nc.Block())

                def tile(t):
                    return z[:, t, 1:S + 1]

                def chunks(ap):
                    return ap.rearrange("p (c t) -> p c t", t=CHUNK)

                @block.gpsimd
                def _(eng):
                    ph.clear(eng)
                    ka = cols("rwkv_k_a", 2)
                    eng.wait_ge(oka_done, 1)
                    for c in range(4):
                        t = c % 2
                        if c >= 2:
                            eng.wait_ge(f_done, 4 * (c - 1))
                        eng.tensor_scalar(km[:, c % 2, :], a[:, c, :], ka[:, t:t + 1], oka[:, t:t + 1], ALU.mult, ALU.add)\
                           .then_inc(km1, 1)
                        eng.tensor_tensor(ba[:, c % 2, :], kk[:, t, :], a[:, c, :], ALU.mult).then_inc(ba_done, 1)
                        eng.wait_ge(km1, c + 1)
                        eng.tensor_tensor(km[:, c % 2, :], km[:, c % 2, :], tile(2 + t), ALU.mult).then_inc(km2, 1)

                @block.tensor
                def _(eng):
                    for t in (0, 1):
                        for j in range(4):
                            mm = eng.transpose(ps[t][:, j * P:(j + 1) * P], z[:, 4 + t, 1 + j * P:1 + (j + 1) * P], k.ident)
                        mm.then_inc(vturned, 1)

                @block.scalar
                def _(eng):
                    for t in (0, 1):
                        eng.wait_ge(vturned, t + 1)
                        eng.activation(vt[:, :, t * P:(t + 1) * P], ps[t][:, :].rearrange("p (j f) -> p j f", j=4),
                                       ACT.Copy).then_inc(vcopied, 1)
                    for c in range(4):
                        if c >= 2:
                            eng.wait_ge(f_done, 4 * (c - 1))
                        eng.wait_ge(l_ref, c + 1)
                        eng.activation(En[:, c % 2, :], L[:, c % 2, :], ACT.Exp, scale=-1.0).then_inc(e_neg, 1)
                        if c < 2:
                            eng.activation(Ep[:, c % 2, :], L[:, c % 2, :], ACT.Exp).then_inc(e_in, 1)
                        eng.wait_ge(l_ex, c + 1)
                        eng.activation(Ee[:, c % 2, :], Le[:, c % 2, :], ACT.Exp).then_inc(e_ex, 1)
                    eng.wait_ge(rsum, 2)
                    eng.activation(carry[:, 0:2, 0:NCH - 1], carry[:, 0:2, 0:NCH - 1], ACT.Exp).then_inc(c_done, 1)
                    eng.activation(carry[:, 2:4, 1:NCH], carry[:, 2:4, 1:NCH], ACT.Exp).then_inc(c_done, 1)

                @block.vector
                def _(eng):
                    eng.tensor_scalar(oka[:, :], cols("rwkv_k_a", 2), -1.0, 1.0, ALU.mult, ALU.add).then_inc(oka_done, 1)

                    def decays(c):
                        d = c // 2
                        if c >= 2:
                            eng.wait_ge(e_neg, c - 1)
                            eng.wait_ge(e_ex, c - 1)
                            eng.wait_ge(e_in, 2)
                        if d == 0:
                            ins = eng.tensor_tensor_scan(L[:, c % 2, :], k.keep_f, lw[:, c, :], 0.0, ALU.mult, ALU.add)
                        else:
                            ins = eng.tensor_tensor_scan(L[:, c % 2, ::-1], k.keep_b[:, ::-1], lw[:, c, ::-1], 0.0,
                                                         ALU.mult, ALU.add)
                        ins.then_inc(scanned, 1)
                        eng.wait_ge(scanned, c + 1)
                        last = CHUNK - 1 if d == 0 else 0
                        eng.tensor_scalar(rho[:, c, :], chunks(L[:, c % 2, :])[:, :, last], 0.5, None, ALU.mult)\
                           .then_inc(rho_done, 1)
                        eng.wait_ge(rho_done, c + 1)
                        ref = rho[:, c, :].unsqueeze(2).to_broadcast([P, NCH, CHUNK])
                        eng.tensor_tensor(chunks(L[:, c % 2, :]), chunks(L[:, c % 2, :]), ref, ALU.subtract)\
                           .then_inc(l_ref, 1)
                        eng.wait_ge(l_ref, c + 1)
                        eng.tensor_tensor(Le[:, c % 2, :], L[:, c % 2, :], lw[:, c, :], ALU.subtract).then_inc(l_ex, 1)

                    decays(0)
                    decays(1)
                    for c in range(4):
                        t = c % 2
                        eng.wait_ge(e_neg, c + 1)
                        eng.wait_ge(e_ex, c + 1)
                        eng.wait_ge(km2, c + 1)
                        eng.wait_ge(ba_done, c + 1)
                        if c == 1:
                            eng.wait_ge(e_in, 2)
                        elif c == 0:
                            eng.wait_ge(e_in, 1)
                        eng.tensor_tensor(feat["K"][:, c, :], km[:, c % 2, :], En[:, c % 2, :], ALU.mult).then_inc(f_done, 1)
                        eng.tensor_tensor(feat["B"][:, c, :], ba[:, c % 2, :], En[:, c % 2, :], ALU.mult).then_inc(f_done, 1)
                        eng.tensor_tensor(feat["A"][:, c, :], kk[:, t, :], Ee[:, c % 2, :], ALU.mult).then_inc(f_done, 1)
                        er = Ep if c < 2 else Ee
                        eng.tensor_tensor(feat["R"][:, c, :], tile(t), er[:, c % 2, :], ALU.mult).then_inc(f_done, 1)
                        if c + 2 < 4:
                            decays(c + 2)
                    eng.wait_ge(rho_done, 4)
                    N1 = NCH - 1
                    eng.tensor_tensor(carry[:, 0:2, 0:N1], rho[:, 0:2, 0:N1], rho[:, 0:2, 1:NCH], ALU.add).then_inc(rsum, 1)
                    eng.tensor_tensor(carry[:, 2:4, 1:NCH], rho[:, 2:4, 0:N1], rho[:, 2:4, 1:NCH], ALU.add).then_inc(rsum, 1)

        Wm = outer.enter_context(nc.sbuf_tensor("rw_W", [P, 4, NCH, 64], F32))
        Qm = outer.enter_context(nc.sbuf_tensor("rw_Q", [P, 4, NCH, 64], F32))
        yl = outer.enter_context(nc.sbuf_tensor("rw_yl", [P, 2, S], F32))
        rwkv_chunks(nc, k, ph, feat, vt, Wm, Qm, yl)
        rwkv_states(nc, k, ph, feat, carry, Wm, Qm, yl)
        norm_features(nc, k, ph, "rwn", yl[:, :, :], [([0], HD), ([1], HD)], k.sum64, k.eps[:, 1:2],
                      cols("rwkv_ln_g", 2), yl[:, :, :], mean=True, bias=cols("rwkv_ln_b", 2))
        rk1, rk2, rk_summed, bonus, added, gated = ph.open(6)
        with ExitStack() as ctx:
            rk = ctx.enter_context(nc.sbuf_tensor("rw_rk", [P, 2, S], F32))
            ps = [ctx.enter_context(nc.psum_tensor(f"rw_pb{i}", [P, 512], F32)) for i in range(2)]
            block = ctx.enter_context(nc.Block())

            @block.gpsimd
            def _(eng):
                ph.clear(eng)

            @block.vector
            def _(eng):
                r_k = cols("rwkv_r_k", 2)
                for t in (0, 1):
                    eng.scalar_tensor_tensor(out=rk[:, t, :], in0=z[:, t, 1:S + 1], scalar=r_k[:, t:t + 1],
                                             in1=z[:, 2 + t, 1:S + 1], op0=ALU.mult, op1=ALU.mult).then_inc(rk1, 1)
                for t in (0, 1):
                    eng.wait_ge(rk_summed, t + 1)
                    eng.tensor_tensor(rk[:, t, :], ps[t][:, :], z[:, 4 + t, 1:S + 1], ALU.mult).then_inc(bonus, 1)
                    eng.wait_ge(bonus, t + 1)
                    eng.tensor_tensor(rk[:, t, :], rk[:, t, :], yl[:, t, :], ALU.add).then_inc(added, 1)
                    eng.wait_ge(added, t + 1)
                    eng.tensor_tensor(o[:, t, :], rk[:, t, :], gate[:, t, :], ALU.mult).then_inc(gated, 1)

            @block.tensor
            def _(eng):
                for t in (0, 1):
                    eng.wait_ge(rk1, t + 1)
                    eng.matmul(ps[t][:, :], k.sum64, rk[:, t, :], start=True, stop=True).then_inc(rk_summed, 1)


def rwkv_chunks(nc, k, ph, feat, vt, Wm, Qm, yl):
    pe_done, v_read, s_read, t_first, mb_done, m_step, halves = ph.open(7)
    order, place = rwkv_plan()
    H = 4
    with ExitStack() as ctx:
        def sb(name, shape):
            return ctx.enter_context(nc.sbuf_tensor(f"rwc_{name}", shape, F32))

        M, MT, NT, RKT, RBT, T, TT, Z = ([sb(f"{n}{d}", [P, H, P]) for d in (0, 1)]
                                         for n in ("M", "MT", "NT", "RKT", "RBT", "T", "TT", "Z"))
        MB = [[sb(f"MB{d}{i}", [P, H, P]) for i in (0, 1)] for d in (0, 1)]
        AG, AU = ([sb(f"{n}{d}", [P, H, P]) for d in (0, 1)] for n in ("AG", "AU"))
        Bt, Kt = ([sb(f"{n}{d}", [P, H, 64]) for d in (0, 1)] for n in ("Bt", "Kt"))
        ps = [ctx.enter_context(nc.psum_tensor(f"rwc_ps{i}", [P, 512], F32)) for i in range(8)]
        block = ctx.enter_context(nc.Block())

        def bank(name, d, b, lv=0):
            return ps[place[name, d, b, lv][0] % 8]

        def heads(ap):
            return ap[:, :].rearrange("p (h c) -> p h c", h=H)

        def made(eng, name, d, b, lv=0):
            eng.wait_ge(pe_done, place[name, d, b, lv][0] + 1)

        def read(eng, name, d, b, lv=0):
            _, reader, n = place[name, d, b, lv]
            eng.wait_ge(v_read if reader == "v" else s_read, n)

        def rows(h):
            return slice(64 * (h % 2), 64 * (h % 2) + 64)

        @block.tensor
        def _(eng):
            def begin(name, d, b, lv=0):
                n = place[name, d, b, lv][0]
                if n >= 8:
                    read(eng, *order[n - 8][:4])
                return bank(name, d, b, lv)

            n_halves = 0

            def other_half(mm):
                nonlocal n_halves
                mm.then_inc(halves, 1)
                n_halves += 1
                eng.wait_ge(halves, n_halves)

            def cross(b, *pair):
                outs = [begin(name, d, b) for name, d, _, _ in pair]
                t = slice(b * P, (b + 1) * P)
                for half in (0, 1):
                    for i in (0, 1):
                        for p, (name, d, left, right) in enumerate(pair):
                            h = 2 * i + (p + half) % 2
                            c = 2 * d + h // 2
                            mm = eng.matmul(outs[p][:, h * P:(h + 1) * P], feat[left][rows(h), c, t],
                                            feat[right][rows(h), c, t], start=True, stop=True)
                            if half and i:
                                mm.then_inc(pe_done, 1)
                    if not half:
                        other_half(mm)

            def per_head(name, d, b, lv, left, right, n=P):
                out = begin(name, d, b, lv)
                for h in range(H):
                    mm = eng.matmul(out[:, h * n:(h + 1) * n], left[:, h, :], right(h), start=True, stop=True)
                mm.then_inc(pe_done, 1)

            for b in range(S // P):
                t = slice(b * P, (b + 1) * P)
                for d in (0, 1):
                    cross(b, ("MT", d, "B", "A"), ("M", d, "A", "B"))
                for d in (0, 1):
                    out = begin("AB", d, b)
                    for i, f in ((0, "A"), (1, "A"), (2, "B"), (3, "B")):
                        mm = eng.transpose(out[:, i * P:(i + 1) * P], feat[f][:, 2 * d + i % 2, t], k.ident)
                    mm.then_inc(pe_done, 1)
                    out = begin("K", d, b)
                    for i in (0, 1):
                        mm = eng.transpose(out[:, i * P:(i + 1) * P], feat["K"][:, 2 * d + i, t], k.ident)
                    mm.then_inc(pe_done, 1)
                cross(b, ("N", 0, "K", "A"), ("N", 1, "K", "A"))
                for lv in range(1, LEVELS + 1):
                    for d in (0, 1):
                        eng.wait_ge(mb_done, 2 * (LEVELS * b + lv - 1) + d + 1)
                        if lv == 1:
                            eng.wait_ge(t_first, 2 * (2 * b + d) + 2)
                        else:
                            read(eng, "X", d, b, lv - 1)
                        per_head("Z", d, b, lv, MB[d][lv % 2], lambda h: T[d][:, h, :])
                    if lv == 1:
                        for d in (0, 1):
                            read(eng, "N", d, b)
                            per_head("G", d, b, 0, NT[d], lambda h: vt[:, b, h * 64:(h + 1) * 64], 64)
                    if lv == 2:
                        cross(b, ("RK", 0, "K", "R"), ("RK", 1, "K", "R"))
                    if lv == 3:
                        cross(b, ("RB", 0, "B", "R"), ("RB", 1, "B", "R"))
                    for d in (0, 1):
                        read(eng, "Z", d, b, lv)
                        if lv > 1:
                            read(eng, "XT", d, b, lv - 1)
                        if lv < LEVELS:
                            per_head("X", d, b, lv, TT[d], lambda h: Z[d][:, h, :])
                        per_head("XT", d, b, lv, Z[d], lambda h: TT[d][:, h, :])
                for d in (0, 1):
                    read(eng, "XT", d, b, LEVELS)
                    read(eng, "G", d, b)
                    per_head("TA", d, b, 0, TT[d], lambda h: AG[d][:, h, :])
                for d in (0, 1):
                    read(eng, "TA", d, b)
                    read(eng, "RB", d, b)
                    out = begin("R", d, b)
                    for h in range(H):
                        c = h // 2 * P
                        mm = eng.matmul(out[rows(h), c:c + P], AU[d][:, h, 0:64], RBT[d][:, h, :], start=True, stop=True)
                    mm.then_inc(pe_done, 1)
                    out = begin("Y", d, b)
                    for h in range(H):
                        c = h // 2 * P
                        eng.matmul(out[rows(h), c:c + P], vt[:, b, h * 64:(h + 1) * 64], RKT[d][:, h, :],
                                   start=True, stop=False)
                        mm = eng.matmul(out[rows(h), c:c + P], AU[d][:, h, 64:P], RBT[d][:, h, :], start=False, stop=True)
                    mm.then_inc(pe_done, 1)
                    pw, pq = begin("W", d, b), begin("Q", d, b)
                    for half in (0, 1):
                        for h in range(H):
                            c = half
                            at, tok = (h // 2 * 2 + c) * 64, slice(64 * c, 64 * c + 64)
                            mm = eng.matmul(pw[rows(h), at:at + 64], AU[d][tok, h, 0:64], Bt[d][tok, h, :],
                                            start=True, stop=True)
                            if half and h == H - 1:
                                mm.then_inc(pe_done, 1)
                            c = 1 - half
                            at, tok = (h // 2 * 2 + c) * 64, slice(64 * c, 64 * c + 64)
                            eng.matmul(pq[rows(h), at:at + 64], Kt[d][tok, h, :], vt[tok, b, h * 64:(h + 1) * 64],
                                       start=True, stop=False)
                            mm = eng.matmul(pq[rows(h), at:at + 64], Bt[d][tok, h, :], AU[d][tok, h, 64:P],
                                            start=False, stop=True)
                        if not half:
                            other_half(mm)
                    mm.then_inc(pe_done, 1)

        @block.gpsimd
        def _(eng):
            ph.clear(eng)
            for b in range(S // P):
                for lv in range(1, LEVELS + 1):
                    for d in (0, 1):
                        read(eng, "MT", d, b)
                        if lv > 2:
                            made(eng, "Z", d, b, lv - 2)
                        elif b > 0:
                            made(eng, "Z", d, b - 1, LEVELS - lv % 2)
                        eng.tensor_tensor(MB[d][lv % 2][:, :, :], MT[d][:, :, :], over_heads(k.between[:, lv, :], H), ALU.mult)\
                           .then_inc(mb_done, 1)

        @block.scalar
        def _(eng):
            for b in range(S // P):
                for d in (0, 1):
                    made(eng, "AB", d, b)
                    if b > 0:
                        made(eng, "Q", d, b - 1)
                    p = bank("AB", d, b)
                    eng.activation(AG[d][:, :, 0:64], p[:, 0:256].rearrange("p (h c) -> p h c", h=H), ACT.Copy)
                    eng.activation(Bt[d][:, :, :], p[:, 256:512].rearrange("p (h c) -> p h c", h=H), ACT.Copy, scale=-1.0)\
                       .then_inc(s_read, 1)
                    made(eng, "K", d, b)
                    eng.activation(Kt[d][:, :, :], bank("K", d, b)[:, 0:256].rearrange("p (h c) -> p h c", h=H), ACT.Copy)\
                       .then_inc(s_read, 1)
                for lv in range(1, LEVELS + 1):
                    for d in (0, 1):
                        made(eng, "Z", d, b, lv)
                        if lv > 1:
                            made(eng, "XT", d, b, lv - 1)
                        elif b > 0:
                            made(eng, "XT", d, b - 1, LEVELS)
                        eng.activation(Z[d][:, :, :], heads(bank("Z", d, b, lv)), ACT.Copy).then_inc(s_read, 1)
                    if lv == 1:
                        for d in (0, 1):
                            made(eng, "G", d, b)
                            eng.activation(AG[d][:, :, 64:P], bank("G", d, b)[:, 0:256].rearrange("p (h c) -> p h c", h=H),
                                           ACT.Copy).then_inc(s_read, 1)
                for d in (0, 1):
                    made(eng, "TA", d, b)
                    eng.activation(AU[d][:, :, :], heads(bank("TA", d, b)), ACT.Copy).then_inc(s_read, 1)
                for d in (0, 1):
                    made(eng, "Q", d, b)
                    eng.activation(Qm[:, 2 * d:2 * d + 2, 2 * b:2 * b + 2, :],
                                   bank("Q", d, b)[:, 0:256].rearrange("p (t c v) -> p t c v", t=2, c=2), ACT.Copy)\
                       .then_inc(s_read, 1)

        @block.vector
        def _(eng):
            def masked(name, d, b, to, mask, sign=1.0):
                made(eng, name, d, b)
                eng.scalar_tensor_tensor(out=to[:, :, :], in0=heads(bank(name, d, b)), scalar=sign,
                                         in1=over_heads(mask, H), op0=ALU.mult, op1=ALU.mult).then_inc(v_read, 1)

            tri = [(k.upper, k.lower, k.upper_in), (k.lower, k.upper, k.lower)]
            for b in range(S // P):
                for d in (0, 1):
                    before, after, seen = tri[d]
                    if b > 0:
                        eng.wait_ge(mb_done, 2 * LEVELS * b)
                        made(eng, "TA", d, b - 1)
                    masked("MT", d, b, MT[d], before)
                    masked("M", d, b, M[d], after)
                for d in (0, 1):
                    before, after, seen = tri[d]
                    for src, dst, name in ((M, T, "M"), (MT, TT, "MT")):
                        read(eng, name, d, b)
                        eng.scalar_tensor_tensor(out=dst[d][:, :, :], in0=src[d][:, :, :], scalar=-1.0,
                                                 in1=over_heads(k.between[:, 0, :], H), op0=ALU.mult, op1=ALU.mult)\
                           .then_inc(m_step, 1)
                    eng.wait_ge(m_step, 2 * (2 * b + d) + 2)
                    for dst in (T, TT):
                        eng.tensor_tensor(dst[d][:, :, :], dst[d][:, :, :], over_heads(k.ident, H), ALU.add)\
                           .then_inc(t_first, 1)
                    masked("N", d, b, NT[d], before)
                for lv in range(1, LEVELS + 1):
                    if lv == 2:
                        for d in (0, 1):
                            masked("RK", d, b, RKT[d], tri[d][2])
                    if lv == 3:
                        for d in (0, 1):
                            masked("RB", d, b, RBT[d], tri[d][2], -1.0)
                    for d in (0, 1):
                        if lv == 1:
                            eng.wait_ge(t_first, 2 * (2 * b + d) + 2)
                        if lv < LEVELS:
                            made(eng, "X", d, b, lv)
                            if lv > 1:
                                read(eng, "X", d, b, lv - 1)
                            eng.tensor_tensor(T[d][:, :, :], T[d][:, :, :], heads(bank("X", d, b, lv)), ALU.subtract)\
                               .then_inc(v_read, 1)
                        made(eng, "XT", d, b, lv)
                        if lv > 1:
                            read(eng, "XT", d, b, lv - 1)
                        eng.tensor_tensor(TT[d][:, :, :], TT[d][:, :, :], heads(bank("XT", d, b, lv)), ALU.subtract)\
                           .then_inc(v_read, 1)
                for d in (0, 1):
                    t = slice(b * P, (b + 1) * P)
                    both = slice(2 * d, 2 * d + 2)
                    made(eng, "R", d, b)
                    eng.tensor_tensor(feat["R"][:, both, t], bank("R", d, b)[:, 0:256].rearrange("p (t c) -> p t c", t=2),
                                      feat["R"][:, both, t], ALU.add).then_inc(v_read, 1)
                    made(eng, "Y", d, b)
                    py = bank("Y", d, b)[:, 0:256].rearrange("p (t c) -> p t c", t=2)
                    if d == 0:
                        eng.tensor_copy(yl[:, :, t], py).then_inc(v_read, 1)
                    else:
                        read(eng, "Y", 0, b)
                        eng.tensor_tensor(yl[:, :, t], py, yl[:, :, t], ALU.add).then_inc(v_read, 1)
                    made(eng, "W", d, b)
                    eng.tensor_tensor(Wm[:, both, 2 * b:2 * b + 2, :],
                                      bank("W", d, b)[:, 0:256].rearrange("p (t c v) -> p t c v", t=2, c=2),
                                      k.eye64.unsqueeze(1).unsqueeze(1).to_broadcast([P, 2, 2, 64]), ALU.add)\
                       .then_inc(v_read, 1)


def rwkv_states(nc, k, ph, feat, carry, Wm, Qm, yl):
    moved, q_added, s_ready, y_made, y_done = ph.open(5)
    with ExitStack() as ctx:
        st = ctx.enter_context(nc.sbuf_tensor("rws_st", [P, 4, NCH, 64], F32))
        tmp = ctx.enter_context(nc.sbuf_tensor("rws_tmp", [P, 4, 64], F32))
        ps = [ctx.enter_context(nc.psum_tensor(f"rws_ps{i}", [P, 512], F32)) for i in range(2)]
        py = [ctx.enter_context(nc.psum_tensor(f"rws_py{i}", [P, 512], F32)) for i in range(2)]
        block = ctx.enter_context(nc.Block())

        @block.gpsimd
        def _(eng):
            ph.clear(eng)

        @block.vector
        def _(eng):
            def at(d, i):
                return i if d == 0 else NCH - 1 - i

            for i in range(NCH - 1):
                if i > 0:
                    eng.wait_ge(moved, i)
                for d in (0, 1):
                    c, both = at(d, i), slice(2 * d, 2 * d + 2)
                    if i == 0:
                        eng.tensor_copy(tmp[:, both, :], Qm[:, both, c, :]).then_inc(q_added, 1)
                    else:
                        pc = ps[i % 2][:, 128 * d:128 * d + 128].rearrange("p (t v) -> p t v", t=2)
                        eng.tensor_tensor(tmp[:, both, :], pc, Qm[:, both, c, :], ALU.add).then_inc(q_added, 1)
                eng.wait_ge(q_added, 2 * i + 2)
                for d in (0, 1):
                    c, n, both = at(d, i), at(d, i + 1), slice(2 * d, 2 * d + 2)
                    e = carry[:, both, c].unsqueeze(2).to_broadcast([P, 2, 64])
                    eng.tensor_tensor(st[:, both, n, :], tmp[:, both, :], e, ALU.mult).then_inc(s_ready, 1)
                eng.wait_ge(s_ready, 2 * i + 2)
            for t in (0, 1):
                eng.wait_ge(y_made, t + 1)
                eng.tensor_tensor(yl[:, t, :], py[t][:, :], yl[:, t, :], ALU.add).then_inc(y_done, 1)

        @block.tensor
        def _(eng):
            for i in range(1, NCH - 1):
                eng.wait_ge(s_ready, 2 * i)
                for d in (0, 1):
                    c = i if d == 0 else NCH - 1 - i
                    for h in range(4):
                        r, q = slice(64 * (h % 2), 64 * (h % 2) + 64), 2 * d + h // 2
                        mm = eng.matmul(ps[i % 2][r, q * 64:(q + 1) * 64], Wm[r, q, c, :], st[r, q, c, :],
                                        start=True, stop=True)
                mm.then_inc(moved, 1)
            eng.wait_ge(s_ready, 2 * (NCH - 1))
            for t in (0, 1):
                for c in range(NCH):
                    tok = slice(c * 64, c * 64 + 64)
                    for p in (0, 1):
                        r = slice(64 * p, 64 * p + 64)
                        dirs = [d for d in (0, 1) if not (d == 0 and c == 0) and not (d == 1 and c == NCH - 1)]
                        for d in dirs:
                            mm = eng.matmul(py[t][r, tok], st[r, 2 * d + t, c, :], feat["R"][r, 2 * d + t, tok],
                                            start=(d == dirs[0]), stop=(d == dirs[-1]))
                mm.then_inc(y_made, 1)


def pooling(nc, k, ph, l, u, o):
    PAD = 16
    loaded, padded, doubled, meant, edged, pooled, mixed, scaled = ph.open(8)
    with ExitStack() as ctx:
        def sb(name, shape):
            return ctx.enter_context(nc.sbuf_tensor(f"pool_{name}", shape, F32))

        sums = sb("sums", [P, 4, 2, PAD + S])
        res = sb("res", [P, 2, S])
        edge = sb("edge", [P, 2, PAD])
        w = sb("w", [P, 2, 64])
        table = sb("counts", [P, 2, PAD + 1])
        ps = [ctx.enter_context(nc.psum_tensor(f"pool_ps{i}", [P, 512], F32)) for i in range(2)]
        block = ctx.enter_context(nc.Block())

        @block.sync
        def _(eng):
            src = k.inp["pool_w_2"][bass.ds(l, 1), :, :, :].rearrange("a (t g) c d -> (a g c) t d", t=2)
            eng.dma_start(w[:, :, :], src).then_inc(loaded, 16)
            eng.dma_start(table[:, :, :], k.pool_table).then_inc(loaded, 16)

        @block.gpsimd
        def _(eng):
            ph.clear(eng)
            eng.memset(u[:, :, 0:PAD], 0.0).then_inc(padded, 1)

        @block.vector
        def _(eng):
            eng.wait_ge(padded, 1)
            last = u
            for i, win in enumerate(POOL_WINDOWS):
                eng.tensor_tensor(sums[:, i, :, win - 1:], last[:, :, win - 1:], last[:, :, win - 1 - win // 2:PAD + S - win // 2],
                                  ALU.add).then_inc(doubled, 1)
                eng.wait_ge(doubled, i + 1)
                last = sums[:, i, :, :]
            eng.wait_ge(loaded, 32)
            for g in range(4):
                r, t = slice(64 * (g % 2), 64 * (g % 2) + 64), g // 2
                eng.tensor_tensor(edge[r, t, :], sums[r, g, t, PAD:2 * PAD], table[r, t, 0:PAD], ALU.mult).then_inc(edged, 1)
                eng.scalar_tensor_tensor(out=res[r, t, PAD:S], in0=sums[r, g, t, 2 * PAD:], scalar=table[r, t, PAD:PAD + 1],
                                         in1=u[r, t, 2 * PAD:], op0=ALU.mult, op1=ALU.subtract).then_inc(pooled, 1)
            eng.wait_ge(edged, 4)
            for t in (0, 1):
                eng.tensor_tensor(res[:, t, 0:PAD], edge[:, t, :], u[:, t, PAD:2 * PAD], ALU.subtract).then_inc(pooled, 1)
            at = AT_2["pool_scale_2"]
            for t in (0, 1):
                eng.wait_ge(mixed, t + 1)
                eng.tensor_scalar(o[:, t, :], ps[t][:, :], k.vec2[:, at + t:at + t + 1], None, ALU.mult).then_inc(scaled, 1)

        @block.tensor
        def _(eng):
            eng.wait_ge(pooled, 6)
            for t in (0, 1):
                for p in (0, 1):
                    r = slice(64 * p, 64 * p + 64)
                    mm = eng.matmul(ps[t][r, :], w[r, t, :], res[r, t, :], start=True, stop=True)
                mm.then_inc(mixed, 1)


def difference_attention(nc, k, ph, l, zq, zk, zv, o):
    H, QK = 4, 64
    SCALE = QK ** -0.5
    with ExitStack() as outer:
        def sb(name, shape):
            return outer.enter_context(nc.sbuf_tensor(f"dif_{name}", shape, F32))

        v = sb("v", [P, 4, H * P])
        neg_lam = sb("neg_lam", [P, 1])
        gain = sb("gain", [P, 4])
        loaded, vturned, vcopied, multiplied, reduced, exped, subbed, lam_done, gained = ph.open(9)
        with ExitStack() as ctx:
            def sb(name, shape):
                return ctx.enter_context(nc.sbuf_tensor(f"dif_{name}", shape, F32))

            lqk = sb("lqk", [P, 4, 64])
            prod = sb("prod", [P, 2, 64])
            dots = sb("dots", [P, 2])
            init = sb("init", [P, 2])
            ps = [ctx.enter_context(nc.psum_tensor(f"dif_pv{i}", [P, 512], F32)) for i in range(4)]
            block = ctx.enter_context(nc.Block())

            @block.sync
            def _(eng):
                for i, n in enumerate(("diff_lq1_2", "diff_lk1_2", "diff_lq2_2", "diff_lk2_2")):
                    eng.dma_start(lqk[:, i, :], bcast_rows(k.inp[n][bass.ds(l, 1), :], P)).then_inc(loaded, 16)
                eng.dma_start(init[:, :], bcast_rows(k.lambda_table[bass.ds(l, 1), :], P)).then_inc(loaded, 16)

            @block.gpsimd
            def _(eng):
                ph.clear(eng)

            @block.tensor
            def _(eng):
                for h in range(H):
                    for j in range(4):
                        mm = eng.transpose(ps[h][:, j * P:(j + 1) * P], zv[:, h, j * P:(j + 1) * P], k.ident)
                    mm.then_inc(vturned, 1)

            @block.scalar
            def _(eng):
                eng.wait_ge(reduced, 2)
                eng.activation(dots[:, :], dots[:, :], ACT.Exp).then_inc(exped, 1)
                for h in range(H):
                    eng.wait_ge(vturned, h + 1)
                    eng.activation(v[:, :, h * P:(h + 1) * P], ps[h][:, :].rearrange("p (j f) -> p j f", j=4), ACT.Copy)\
                       .then_inc(vcopied, 1)

            @block.vector
            def _(eng):
                eng.wait_ge(loaded, 80)
                for i in (0, 1):
                    eng.tensor_tensor(prod[:, i, :], lqk[:, 2 * i, :], lqk[:, 2 * i + 1, :], ALU.mult).then_inc(multiplied, 1)
                for i in (0, 1):
                    eng.wait_ge(multiplied, i + 1)
                    eng.tensor_reduce(dots[:, i:i + 1], prod[:, i, :], AX, ALU.add).then_inc(reduced, 1)
                eng.wait_ge(exped, 1)
                eng.tensor_tensor(neg_lam[:, :], dots[:, 1:2], dots[:, 0:1], ALU.subtract).then_inc(subbed, 1)
                eng.wait_ge(subbed, 1)
                eng.tensor_tensor(neg_lam[:, :], neg_lam[:, :], init[:, 0:1], ALU.subtract).then_inc(lam_done, 1)
                at = AT_2["diff_norm_g_2"]
                eng.tensor_scalar(gain[:, :], k.vec2[:, at:at + 4], init[:, 1:2], None, ALU.mult).then_inc(gained, 1)

        (scored, maxed, nm_ready, exp_done, inv_done, c_done, second, combined, a_turned, a_copied, o_made,
         o_copied) = ph.open(12)
        with ExitStack() as ctx:
            def sb(name, shape):
                return ctx.enter_context(nc.sbuf_tensor(f"dif_{name}", shape, F32))

            prob = sb("prob", [P, 2, 2, 4, S])
            m, nm, rs, rr = (sb(n, [P, 2, 8]) for n in ("m", "nm", "rs", "rr"))
            pt = sb("pt", [P, 2, S])
            ps = [ctx.enter_context(nc.psum_tensor(f"dif_ps{i}", [P, 512], F32)) for i in range(4)]
            pp = [ctx.enter_context(nc.psum_tensor(f"dif_pp{i}", [P, 512], F32)) for i in range(2)]
            po = [ctx.enter_context(nc.psum_tensor(f"dif_po{i}", [P, 512], F32)) for i in range(2)]
            block = ctx.enter_context(nc.Block())
            B = len(ps)

            def units(h):
                return [(8 * h + 4 * mp + i, mp, i, (i + 1) * P) for mp in (0, 1) for i in range(4)]

            @block.gpsimd
            def _(eng):
                ph.clear(eng)

            @block.tensor
            def _(eng):
                def scores(h):
                    for u, mp, i, n in units(h):
                        if u >= B:
                            eng.wait_ge(exp_done, u - B + 1)
                        r = slice(64 * mp, 64 * mp + 64)
                        eng.matmul(ps[u % B][:, 0:n], zq[r, h, i * P:(i + 1) * P], zk[r, h, 0:n], start=True, stop=False)
                        eng.matmul(ps[u % B][:, n - P:n], k.mask_q[r, :], k.mask_k[r, :], start=False, stop=True)\
                           .then_inc(scored, 1)

                scores(0)
                for h in range(H):
                    if h + 1 < H:
                        scores(h + 1)
                    eng.wait_ge(combined, 4 * (h + 1))

                    def turn(j):
                        u = 4 * h + j
                        if u >= 2:
                            eng.wait_ge(a_copied, u - 1)
                        for i in range(j, 4):
                            mm = eng.transpose(pp[u % 2][:, i * P:(i + 1) * P], prob[:, h % 2, 0, i, j * P:(j + 1) * P], k.ident)
                        mm.then_inc(a_turned, 1)

                    turn(0)
                    if h >= 2:
                        eng.wait_ge(o_copied, h - 1)
                    for j in range(4):
                        if j < 3:
                            turn(j + 1)
                        u = 4 * h + j
                        eng.wait_ge(a_copied, u + 1)
                        eng.matmul(po[h % 2][:, j * P:S], v[:, j, h * P:(h + 1) * P], pt[:, u % 2, j * P:S],
                                   start=(j == 0), stop=(j == 3)).then_inc(o_made, 1)

            @block.scalar
            def _(eng):
                def exps(h):
                    for u, mp, i, n in units(h):
                        eng.wait_ge(nm_ready, u + 1)
                        if h >= 2:
                            eng.wait_ge(a_turned, 4 * (h - 1))
                            eng.wait_ge(combined, 4 * (h - 1))
                        c = 4 * mp + i
                        eng.activation(prob[:, h % 2, mp, i, 0:n], ps[u % B][:, 0:n], ACT.Exp, scale=SCALE,
                                       bias=nm[:, h % 2, c:c + 1], accum_out=rs[:, h % 2, c:c + 1]).then_inc(exp_done, 1)

                exps(0)
                for h in range(H):
                    if h + 1 < H:
                        exps(h + 1)
                    for j in range(4):
                        u = 4 * h + j
                        eng.wait_ge(a_turned, u + 1)
                        if u >= 2:
                            eng.wait_ge(o_made, u - 1)
                        eng.activation(pt[:, u % 2, j * P:S], pp[u % 2][:, j * P:S], ACT.Copy).then_inc(a_copied, 1)
                    eng.wait_ge(o_made, 4 * (h + 1))
                    eng.activation(o[:, h, :], po[h % 2][:, :], ACT.Copy).then_inc(o_copied, 1)

            @block.vector
            def _(eng):
                def maxes(h):
                    for u, mp, i, n in units(h):
                        c = 4 * mp + i
                        eng.wait_ge(scored, u + 1)
                        if h >= 2:
                            eng.wait_ge(exp_done, 8 * (h - 1))
                        eng.tensor_reduce(m[:, h % 2, c:c + 1], ps[u % B][:, 0:n], AX, ALU.max).then_inc(maxed, 1)
                        eng.wait_ge(maxed, u + 1)
                        eng.tensor_scalar(nm[:, h % 2, c:c + 1], m[:, h % 2, c:c + 1], -SCALE, None, ALU.mult)\
                           .then_inc(nm_ready, 1)

                maxes(0)
                for h in range(H):
                    b = h % 2
                    eng.wait_ge(exp_done, 8 * (h + 1))
                    eng.reciprocal(rr[:, b, :], rs[:, b, :]).then_inc(inv_done, 1)
                    eng.wait_ge(inv_done, h + 1)
                    eng.tensor_scalar(rr[:, b, 4:8], rr[:, b, 4:8], neg_lam[:, 0:1], None, ALU.mult).then_inc(c_done, 1)
                    eng.wait_ge(c_done, h + 1)
                    for i in range(4):
                        n = (i + 1) * P
                        eng.tensor_scalar(prob[:, b, 1, i, 0:n], prob[:, b, 1, i, 0:n], rr[:, b, 4 + i:5 + i], None, ALU.mult)\
                           .then_inc(second, 1)
                        eng.wait_ge(second, 4 * h + i + 1)
                        eng.scalar_tensor_tensor(out=prob[:, b, 0, i, 0:n], in0=prob[:, b, 0, i, 0:n], scalar=rr[:, b, i:i + 1],
                                                 in1=prob[:, b, 1, i, 0:n], op0=ALU.mult, op1=ALU.add).then_inc(combined, 1)
                    if h + 1 < H:
                        maxes(h + 1)

        norm_features(nc, k, ph, "difn", o, [([t], P) for t in range(4)], k.ones, k.eps[:, 0:1], gain[:, :], o)


def gated_linear_attention(nc, k, ph, l, zq, zk, zv, zr, zg, o):
    H = 4
    with ExitStack() as outer:
        def sb(name, shape):
            return outer.enter_context(nc.sbuf_tensor(f"gla_{name}", shape, F32))

        qd, ki = sb("qd", [P, S]), sb("ki", [P, S])
        ket, vt = sb("ket", [P, 4, P]), sb("vt", [P, 4, 256])
        ebl = sb("ebl", [P, NCH])
        y = sb("y", [P, 2, S])
        (loaded, g_made, biased, absed, exped, logged, minned, la_done, scanned, endsub, ep_done, en_done, ee_done,
         ke_done, q_done, vturned, vcopied, kturned) = ph.open(18)
        with ExitStack() as ctx:
            def sb(name, shape):
                return ctx.enter_context(nc.sbuf_tensor(f"gla_{name}", shape, F32))

            w = sb("w", [GLA_RANK, P])
            yb, ab, la, L, De = (sb(n, [P, S]) for n in ("yb", "ab", "la", "L", "De"))
            Ep, En, Ee, ke = (sb(n, [P, S]) for n in ("Ep", "En", "Ee", "ke"))
            pg = ctx.enter_context(nc.psum_tensor("gla_pg", [P, 512], F32))
            pk = ctx.enter_context(nc.psum_tensor("gla_pk", [P, 512], F32))
            pv = [ctx.enter_context(nc.psum_tensor(f"gla_pv{i}", [P, 512], F32)) for i in range(2)]
            block = ctx.enter_context(nc.Block())

            def chunks(ap):
                return ap.rearrange("p (c t) -> p c t", t=CHUNK)

            @block.sync
            def _(eng):
                eng.dma_start(w[:, :], k.inp["gla_w_gate2_2"][bass.ds(l, 1), :, :].rearrange("a r c -> (a r) c"))\
                   .then_inc(loaded, 16)

            @block.gpsimd
            def _(eng):
                ph.clear(eng)

            @block.tensor
            def _(eng):
                eng.wait_ge(loaded, 16)
                eng.matmul(pg[:, :], w[:, :], zg, start=True, stop=True).then_inc(g_made, 1)
                for t in (0, 1):
                    for j in range(4):
                        mm = eng.transpose(pv[t][:, j * P:(j + 1) * P], zv[:, t, j * P:(j + 1) * P], k.ident)
                    mm.then_inc(vturned, 1)
                eng.wait_ge(ke_done, 1)
                for j in range(4):
                    mm = eng.transpose(pk[:, j * P:(j + 1) * P], ke[:, j * P:(j + 1) * P], k.ident)
                mm.then_inc(kturned, 1)

            @block.vector
            def _(eng):
                at = AT_2["gla_b_gate_2"]
                eng.wait_ge(g_made, 1)
                eng.tensor_scalar(yb[:, :], pg[:, :], k.vec2[:, at:at + 1], None, ALU.add).then_inc(biased, 1)
                eng.wait_ge(biased, 1)
                eng.scalar_tensor_tensor(out=ab[:, :], in0=yb[:, :], scalar=-1.0, in1=yb[:, :], op0=ALU.mult, op1=ALU.max)\
                   .then_inc(absed, 1)
                eng.tensor_scalar(yb[:, :], yb[:, :], 0.0, None, ALU.min).then_inc(minned, 1)
                eng.wait_ge(minned, 1)
                eng.wait_ge(logged, 1)
                eng.tensor_tensor(la[:, :], yb[:, :], ab[:, :], ALU.subtract).then_inc(la_done, 1)
                eng.wait_ge(la_done, 1)
                eng.tensor_tensor_scan(L[:, :], k.keep_f, la[:, :], 0.0, ALU.mult, ALU.add).then_inc(scanned, 1)
                eng.wait_ge(scanned, 1)
                end = chunks(L[:, :])[:, :, CHUNK - 1:CHUNK].to_broadcast([P, NCH, CHUNK])
                eng.tensor_tensor(chunks(De[:, :]), end, chunks(L[:, :]), ALU.subtract).then_inc(endsub, 1)
                eng.wait_ge(ee_done, 1)
                eng.tensor_tensor(ke[:, :], zk, Ee[:, :], ALU.mult).then_inc(ke_done, 1)
                eng.wait_ge(ep_done, 1)
                eng.scalar_tensor_tensor(out=qd[:, :], in0=zq, scalar=GLA_KD ** -0.5, in1=Ep[:, :], op0=ALU.mult,
                                         op1=ALU.mult).then_inc(q_done, 1)
                eng.wait_ge(en_done, 1)
                eng.tensor_tensor(ki[:, :], zk, En[:, :], ALU.mult).then_inc(q_done, 1)

            @block.scalar
            def _(eng):
                eng.wait_ge(absed, 1)
                eng.activation(ab[:, :], ab[:, :], ACT.Exp, scale=-1.0).then_inc(exped, 1)
                eng.wait_ge(exped, 1)
                eng.activation(ab[:, :], ab[:, :], ACT.Ln, bias=k.ones[:, 0:1]).then_inc(logged, 1)
                eng.wait_ge(endsub, 1)
                eng.activation(Ee[:, :], De[:, :], ACT.Exp, scale=1.0 / GLA_TAU).then_inc(ee_done, 1)
                eng.activation(Ep[:, :], L[:, :], ACT.Exp, scale=1.0 / GLA_TAU).then_inc(ep_done, 1)
                eng.activation(En[:, :], L[:, :], ACT.Exp, scale=-1.0 / GLA_TAU).then_inc(en_done, 1)
                eng.activation(ebl[:, :], chunks(L[:, :])[:, :, CHUNK - 1], ACT.Exp, scale=1.0 / GLA_TAU).then_inc(en_done, 1)
                for t in (0, 1):
                    eng.wait_ge(vturned, t + 1)
                    eng.activation(vt[:, :, t * P:(t + 1) * P], pv[t][:, :].rearrange("p (j f) -> p j f", j=4), ACT.Copy)\
                       .then_inc(vcopied, 1)
                eng.wait_ge(kturned, 1)
                eng.activation(ket[:, :, :], pk[:, :].rearrange("p (j f) -> p j f", j=4), ACT.Copy).then_inc(vcopied, 1)

        scored, masked, kv_made, s_ready, intra, inter, y_copied, y_added = ph.open(8)
        with ExitStack() as ctx:
            att = ctx.enter_context(nc.sbuf_tensor("gla_att", [P, H, 4, P], F32))
            st = ctx.enter_context(nc.sbuf_tensor("gla_st", [P, NCH, 64], F32))
            pa = [ctx.enter_context(nc.psum_tensor(f"gla_pa{i}", [P, 512], F32)) for i in range(4)]
            pkv = [ctx.enter_context(nc.psum_tensor(f"gla_pkv{i}", [P, 512], F32)) for i in range(2)]
            po = [ctx.enter_context(nc.psum_tensor(f"gla_po{i}", [P, 512], F32)) for i in range(2)]
            block = ctx.enter_context(nc.Block())

            @block.gpsimd
            def _(eng):
                ph.clear(eng)

            @block.tensor
            def _(eng):
                for h in range(H):
                    r = slice(32 * h, 32 * h + 32)
                    for b in range(4):
                        t = slice(b * P, (b + 1) * P)
                        mm = eng.matmul(pa[h][:, t], ki[r, t], qd[r, t], start=True, stop=True)
                    mm.then_inc(scored, 1)
                for p in (0, 1):
                    tok = slice(64 * p, 64 * p + 64)
                    for b in range(4):
                        for h in range(H):
                            mm = eng.matmul(pkv[p][32 * h:32 * h + 32, b * 64:(b + 1) * 64], ket[tok, b, 32 * h:32 * h + 32],
                                            vt[tok, b, h * 64:(h + 1) * 64], start=True, stop=True)
                    mm.then_inc(kv_made, 1)
                for h in range(H):
                    eng.wait_ge(masked, h + 1)
                    r = slice(64 * (h % 2), 64 * (h % 2) + 64)
                    for b in range(4):
                        mm = eng.matmul(po[h // 2][r, b * P:(b + 1) * P], vt[:, b, h * 64:(h + 1) * 64], att[:, h, b, :],
                                        start=True, stop=True)
                    mm.then_inc(intra, 1)
                eng.wait_ge(s_ready, NCH - 1)
                for h in range(H):
                    r = slice(64 * (h % 2), 64 * (h % 2) + 64)
                    rk = slice(32 * h, 32 * h + 32)
                    for c in range(1, NCH):
                        t = slice(c * CHUNK, (c + 1) * CHUNK)
                        mm = eng.matmul(pa[h // 2][r, t], st[rk, c, :], qd[rk, t], start=True, stop=True)
                    mm.then_inc(inter, 1)

            @block.scalar
            def _(eng):
                for t in (0, 1):
                    eng.wait_ge(intra, 2 * t + 2)
                    eng.activation(y[:, t, :], po[t][:, :], ACT.Copy).then_inc(y_copied, 1)

            @block.vector
            def _(eng):
                for h in range(H):
                    eng.wait_ge(scored, h + 1)
                    eng.tensor_tensor(att[:, h, :, :], pa[h][:, :].rearrange("p (b t) -> p b t", b=4),
                                      over_heads(k.upper_in, 4), ALU.mult).then_inc(masked, 1)
                eng.wait_ge(kv_made, 2)
                eng.tensor_copy(st[:, 1, :], pkv[0][:, 0:64]).then_inc(s_ready, 1)
                for c in range(1, NCH - 1):
                    eng.wait_ge(s_ready, c)
                    eng.scalar_tensor_tensor(out=st[:, c + 1, :], in0=st[:, c, :], scalar=ebl[:, c:c + 1],
                                             in1=pkv[c % 2][:, c // 2 * 64:c // 2 * 64 + 64], op0=ALU.mult, op1=ALU.add)\
                       .then_inc(s_ready, 1)
                for t in (0, 1):
                    eng.wait_ge(inter, 2 * t + 2)
                    eng.wait_ge(y_copied, t + 1)
                    eng.tensor_tensor(y[:, t, CHUNK:S], pa[t][:, CHUNK:S], y[:, t, CHUNK:S], ALU.add).then_inc(y_added, 1)

        at = AT_2["gla_norm_g_2"]
        norm_features(nc, k, ph, "glan", y[:, :, :], [([0], HD), ([1], HD)], k.sum64, k.eps[:, 0:1],
                      k.vec2[:, at:at + 2], o, gate=zr)


def mixers_2(nc, k, ph, l):
    with ExitStack() as outer:
        o = outer.enter_context(nc.sbuf_tensor("o2_cols", [P, DT, S], F32))
        with ExitStack() as ctx:
            z_pool = ctx.enter_context(nc.sbuf_tensor("z_pool", [P, 2, 16 + S], F32))[:, :, :]
            z = ctx.enter_context(nc.sbuf_tensor("z_2", [P, 18, S], F32))
            z_gate = ctx.enter_context(nc.sbuf_tensor("z_gate", [GLA_RANK, S], F32))[:, :]
            with operand(nc, "mix2_h", DT) as (hi, lo):
                at = AT_2["norm1_g_2"]
                tiles = [(t * P, P) for t in range(20)] + [(20 * P, GLA_RANK)]

                def store(eng, t, ps):
                    if t < 2:
                        return eng.tensor_copy(z_pool[:, t, 16:16 + S], ps)
                    return eng.tensor_copy(z_gate if t == 20 else z[:, t - 2, :], ps)

                project(nc, k, ph, "in2", l, k.inp["w_in_2"], tiles, hi, lo, store,
                        (k.vec2[:, at:at + DT], None), o)
            pooling(nc, k, ph, l, z_pool, o[:, 0:2, :])
            gated_linear_attention(nc, k, ph, l, z[:, 12, :], z[:, 13, :], z[:, 14:16, :], z[:, 16:18, :], z_gate,
                                   o[:, 6:8, :])
            difference_attention(nc, k, ph, l, z[:, 0:4, :], z[:, 4:8, :], z[:, 8:12, :], o[:, 2:6, :])
        with operand(nc, "o2", DT) as (hi, lo):
            split(nc, k, ph, o, hi, lo, DT)
            add_projected(nc, k, ph, "out2", l, k.inp["w_out_2"], hi, lo, None)


class Chip:
    pass


NAMES = [
    "x", "c", "positions", "w_ada", "b_ada", "w_ff1_in", "w_ff1_out", "w_ff2_in", "w_ff2_out", "w_in", "w_out",
    "rwkv_mu", "rwkv_w0", "rwkv_w_up", "rwkv_a0", "rwkv_a_up", "rwkv_g_up", "rwkv_k_k", "rwkv_k_a", "rwkv_r_k",
    "rwkv_ln_g", "rwkv_ln_b", "mla_q_norm_g", "mla_w_uq", "mla_kv_norm_g", "mla_w_ukv", "ret_log_rate",
    "ret_gn_g", "final_norm_g", "norm1_g_2", "w_in_2", "pool_w_2", "pool_scale_2", "diff_lq1_2", "diff_lk1_2",
    "diff_lq2_2", "diff_lk2_2", "diff_norm_g_2", "gla_w_gate2_2", "gla_b_gate_2", "gla_norm_g_2", "w_out_2",
    "norm2_g_2", "w_mlp1_2", "w_mlp2_2", "final_norm_g_2",
]


def build(nc, inp, consts, out):
    k = Chip()
    k.inp = inp
    k.pool_table, k.lambda_table = consts["pool_table"], consts["lambda_table"]
    k.flat = {}
    for name, _ in VECS_1 + VECS_2:
        a = inp[name]
        dims = " ".join("abcd"[i] for i in range(len(a.shape) - 1))
        k.flat[name] = a if len(a.shape) == 2 else a.rearrange(f"l {dims} -> l ({dims})")
    with ExitStack() as ctx:
        def sb(name, shape, dt=F32):
            t = ctx.enter_context(nc.sbuf_tensor(name, shape, dt))
            return t[tuple(slice(None) for _ in shape)]

        k.x = sb("x_cols", [P, DT, S])
        k.ident = sb("ident", [P, P])
        k.rot64 = sb("rot64", [P, P])
        k.rot32 = sb("rot32", [MLA_QK, MLA_QK])
        k.put32 = sb("put32", [32, MLA_QK])
        k.putrot32 = sb("putrot32", [32, MLA_QK])
        k.sum64 = sb("sum64", [P, P])
        k.ones = sb("ones", [P, P])
        k.upper, k.upper_in, k.lower, k.lower_in = (sb(n, [P, P]) for n in ("upper", "upper_in", "lower", "lower_in"))
        k.keep_f, k.keep_b = sb("keep_f", [P, S]), sb("keep_b", [P, S])
        k.between = sb("between", [P, 6, P])
        k.eye64 = sb("eye64", [P, 64])
        k.mask_q, k.mask_k = sb("mask_q", [P, P]), sb("mask_k", [P, P])
        k.eps = sb("eps", [P, 4])
        k.sin, k.cos = sb("sin", [P, 2, S]), sb("cos", [P, 2, S])
        k.cond = sb("cond", [P, DT])
        k.finals = sb("finals", [P, 2 * DT])
        k.vec1, k.vec2 = sb("vec1", [P, N_VEC_1]), sb("vec2", [P, N_VEC_2])
        k.mod, k.mod_next, k.half_b = sb("mod", [P, 9 * DT]), sb("mod_next", [P, 3 * DT]), sb("half_b", [P, 2 * DT])

        ph = Phases(nc, ctx, 30)
        constants(nc, k, ph, consts["inv_freq"])

        def mod(j):
            return k.mod[:, j * DT:(j + 1) * DT]

        ahead = list(range(3 * DT))
        beside = list(range(3 * DT, 9 * DT))

        def keep_sums(eng, at, ps):
            return eng.tensor_copy(k.mod_next[:, at:at + 4], ps)

        def finished(eng, cols, src):
            group = cols.start // DT
            b = k.vec1[:, AT_1["b_ada"] + cols.start:AT_1["b_ada"] + cols.stop]
            if group % 3 == 1:
                return eng.scalar_tensor_tensor(out=k.mod[:, cols], in0=src, scalar=1.0, in1=b, op0=ALU.add, op1=ALU.add)
            if group in (2, 8):
                h = k.half_b[:, (group // 6) * DT + cols.start % DT:][:, :cols.stop - cols.start]
                return eng.scalar_tensor_tensor(out=k.mod[:, cols], in0=src, scalar=0.5, in1=h, op0=ALU.mult, op1=ALU.add)
            return eng.tensor_tensor(k.mod[:, cols], src, b, ALU.add)

        def finish_sums(eng, at, ps):
            return finished(eng, slice(3 * DT + at, 3 * DT + at + 4), ps)

        def start_layer(done):
            def also(eng):
                for i, group in enumerate((2, 8)):
                    b = k.vec1[:, AT_1["b_ada"] + group * DT:AT_1["b_ada"] + (group + 1) * DT]
                    eng.tensor_scalar(k.half_b[:, i * DT:(i + 1) * DT], b, 0.5, None, ALU.mult).then_inc(done[0], 1)
                eng.wait_ge(done[0], 2)
                for group in range(3):
                    cols = slice(group * DT, (group + 1) * DT)
                    finished(eng, cols, k.mod_next[:, cols])
            return also

        first_modulation(nc, k, ph, 0, ahead, keep_sums)
        first = ph.turn

        def mod(j):
            return k.mod[:, j * DT:(j + 1) * DT]

        with nc.Fori(0, DEPTH) as l:
            load_vectors(nc, k, ph, l, VECS_1, N_VEC_1, k.vec1, start_layer)
            feed_forward(nc, k, ph, "f1", l, inp["w_ff1_in"], inp["w_ff1_out"], D_FF, 11, True,
                         (mod(1), mod(0)), mod(2), (l, beside, finish_sums))
            mixers_1(nc, k, ph, l, mod)
            feed_forward(nc, k, ph, "f2", l, inp["w_ff2_in"], inp["w_ff2_out"], D_FF, 11, True,
                         (mod(7), mod(6)), mod(8), ((l + 1) % DEPTH, ahead, keep_sums))
            even(nc, ph, first)
        normalise(nc, k, ph, "nf1", k.finals[:, 0:DT])
        first = ph.turn
        with nc.Fori(0, DEPTH) as l:
            load_vectors(nc, k, ph, l, VECS_2, N_VEC_2, k.vec2)
            mixers_2(nc, k, ph, l)
            at = AT_2["norm2_g_2"]
            feed_forward(nc, k, ph, "mlp", l, inp["w_mlp1_2"], inp["w_mlp2_2"], D_MLP, 8, False,
                         (k.vec2[:, at:at + DT], None), None)
            even(nc, ph, first)
        normalise(nc, k, ph, "nf2", k.finals[:, DT:2 * DT])
        finish(nc, k, ph, out)


def even(nc, ph, first):
    if ph.turn != first:
        ph.open(0)
        with nc.Block() as block:
            @block.gpsimd
            def _(eng):
                ph.clear(eng)


class operand:

    def __init__(self, nc, name, n):
        self.nc, self.name, self.n = nc, name, n

    def __enter__(self):
        self.ctx = ExitStack()
        return [self.ctx.enter_context(self.nc.sbuf_tensor(f"{self.name}_{part}", [P, self.n, S], F32R))
                for part in ("hi", "lo")]

    def __exit__(self, *failure):
        if failure[0] is None:
            self.ctx.close()


def inverse_frequencies():
    import numpy as np
    table = np.zeros((P, 2), np.float32)
    mla = np.float32(ROPE_BASE) ** (-np.arange(0, MLA_ROPE, 2, dtype=np.float32) / np.float32(MLA_ROPE))
    ret = np.float32(ROPE_BASE) ** (-np.arange(0, HD, 2, dtype=np.float32) / np.float32(HD))
    table[64:96, 0] = np.tile(mla, 2)
    table[:, 1] = np.tile(ret, 4)
    return table


def pool_counts():
    import numpy as np
    table = np.zeros((P, 2, 17), np.float32)
    for g, win in enumerate(POOL_WINDOWS):
        rows = slice(64 * (g % 2), 64 * (g % 2) + 64)
        table[rows, g // 2, :16] = 1.0 / np.minimum(np.arange(16) + 1, win)
        table[rows, g // 2, 16] = 1.0 / win
    return table


def lambda_inits():
    import math
    import numpy as np
    init = [0.8 - 0.6 * math.exp(-0.3 * i) for i in range(DEPTH)]
    return np.array([[v, 1.0 - v] for v in init], np.float32)


CONSTANTS = {"inv_freq": inverse_frequencies, "pool_table": pool_counts, "lambda_table": lambda_inits}


def kernel(**inputs):
    import numpy as np
    import concourse.bacc as bacc
    from concourse.bass_utils import run_bass_kernel_spmd

    nc = bacc.Bacc("TRN2", target_bir_lowering=False, num_devices=1)
    arrays, inp = {}, {}
    for name in NAMES:
        a = np.ascontiguousarray(inputs[name])
        arrays[f"in_{name}"] = a
        inp[name] = nc.dram_tensor(f"in_{name}", a.shape, mybir.dt.from_np(a.dtype), kind="ExternalInput").ap()
    consts = {}
    for name, table in CONSTANTS.items():
        arrays[name] = table()
        consts[name] = nc.dram_tensor(name, arrays[name].shape, F32, kind="ExternalInput").ap()
    out = nc.dram_tensor("out_x", (1, S, D), F32, kind="ExternalOutput").ap()
    build(nc, inp, consts, out)
    r = run_bass_kernel_spmd(nc, [arrays], core_ids=[0])
    return r.results[0]["out_x"]
```
